# Optimizing a Trainium2 kernel written in Bass

```python
import math
import jax, jax.numpy as jnp
from jax import lax
import numpy as np

D_MODEL = 1024
BATCH = 1
SEQ = 1024
DEPTH = 1
DEC_BATCH = 8
DEC_SEQ = 8
PAST_LEN = 2048
PAGE_SIZE = 128

HEAD_DIM = 64
N_ATT_HEADS = 12
ATT_WIDTH = N_ATT_HEADS * HEAD_DIM
CONV_WIDTH = D_MODEL - ATT_WIDTH
MIX_WIDTH = ATT_WIDTH + CONV_WIDTH
CONV_K = 31
DILATED_BRANCHES = ((128, 1), (512, 4), (2048, 16))
MAX_WINDOW = 2048
N_BUCKETS = 32
MAX_EXACT = N_BUCKETS // 2
MAX_DISTANCE = 2048
N_MEM = 256
X_HEADS = 4
X_HEAD_DIM = D_MODEL // X_HEADS
D_FF = -(-(8 * D_MODEL) // (3 * 256)) * 256
EPS = 1e-6
ATT_SCALE = HEAD_DIM ** -0.5
X_SCALE = X_HEAD_DIM ** -0.5

kernel_name = 'hybrid_dilated_conformer_decoder_step'

def rmsnorm(x, g):
    xf = x.astype(jnp.float32)
    xf = xf * lax.rsqrt(jnp.mean(xf * xf, axis=-1, keepdims=True) + EPS)
    return (xf * g.astype(jnp.float32)).astype(x.dtype)

def layernorm(x, g, b):
    xf = x.astype(jnp.float32)
    mu = jnp.mean(xf, axis=-1, keepdims=True)
    xc = xf - mu
    var = jnp.mean(xc * xc, axis=-1, keepdims=True)
    return (xc * lax.rsqrt(var + EPS) * g.astype(jnp.float32) + b.astype(jnp.float32)).astype(x.dtype)

def t5_bucket(dist):
    n = dist.astype(jnp.int32)
    nf = jnp.maximum(n, MAX_EXACT).astype(jnp.float32)
    large = MAX_EXACT + (jnp.log(nf / MAX_EXACT) / math.log(MAX_DISTANCE / MAX_EXACT)
                         * (N_BUCKETS - MAX_EXACT)).astype(jnp.int32)
    large = jnp.minimum(large, N_BUCKETS - 1)
    return jnp.where(n < MAX_EXACT, n, large)

def rel_bias(table, dist):
    return jnp.moveaxis(table[t5_bucket(dist)], -1, 0).astype(jnp.float32)

def masked_softmax_stats(s, valid):
    s = jnp.where(valid, s, -jnp.inf)
    m = jnp.max(s, axis=-1, keepdims=True)
    p = jnp.exp(s - m)
    den = jnp.sum(p, axis=-1, keepdims=True)
    return p / den, (m + jnp.log(den))[..., 0]

def combine_branches(outs, lses):
    lse = jnp.stack(lses, 0)
    w = jnp.exp(lse - jnp.max(lse, axis=0, keepdims=True))
    w = w / jnp.sum(w, axis=0, keepdims=True)
    o = jnp.sum(w[..., None] * jnp.stack(outs, 0).astype(jnp.float32), axis=0)
    return o.astype(outs[0].dtype)

def dilated_branch_prompt(q, k, v, table, dilation, steps):
    S, H, hd = q.shape
    L = S // dilation
    nb = -(-L // steps)
    Lp = nb * steps

    def to_blocks(t):
        t = t.reshape(L, dilation, H, hd).transpose(1, 0, 2, 3)
        t = jnp.pad(t, ((0, 0), (0, Lp - L), (0, 0), (0, 0)))
        return t.reshape(dilation, nb, steps, H, hd)

    def with_prev(t):
        prev = jnp.pad(t[:, :-1], ((0, 0), (1, 0), (0, 0), (0, 0), (0, 0)))
        return jnp.concatenate([prev, t], axis=2)

    qb = to_blocks(q)
    kk = with_prev(to_blocks(k))
    vv = with_prev(to_blocks(v))
    qi = jnp.arange(steps)[:, None]
    kj = jnp.arange(2 * steps)[None, :]
    sub_dist = steps + qi - kj
    band = (sub_dist >= 0) & (sub_dist <= steps)
    blk = jnp.arange(nb)[:, None, None]
    valid = band[None] & (blk * steps + kj[None] - steps >= 0)
    bias = rel_bias(table, dilation * jnp.maximum(sub_dist, 0))
    s = jnp.einsum('gnqhd,gnkhd->gnhqk', qb, kk).astype(jnp.float32) * ATT_SCALE + bias[None, None]
    p, lse = masked_softmax_stats(s, valid[None, :, None])
    o = jnp.einsum('gnhqk,gnkhd->gnqhd', p.astype(v.dtype), vv)
    o = o.reshape(dilation, Lp, H, hd)[:, :L].transpose(1, 0, 2, 3).reshape(S, H, hd)
    lse = lse.transpose(0, 1, 3, 2).reshape(dilation, Lp, H)[:, :L].transpose(1, 0, 2).reshape(S, H)
    return o, lse

def dilated_attention_prompt(q, k, v, table):
    def one(args):
        qs, ks, vs = args
        outs, lses = [], []
        for window, dil in DILATED_BRANCHES:
            o, l = dilated_branch_prompt(qs, ks, vs, table, dil, window // dil)
            outs.append(o)
            lses.append(l)
        return combine_branches(outs, lses)
    return lax.map(one, (q, k, v))

def dilated_attention_sample(q, kc, vc, table, buf_len):
    T = q.shape[1]
    outs, lses = [], []
    for window, dil in DILATED_BRANCHES:
        steps = window // dil
        i = jnp.arange(T)[:, None]
        j = jnp.arange(steps + 1)
        idx = buf_len + i - j[None, :] * dil
        valid = idx >= 0
        idxc = jnp.maximum(idx, 0)
        kg = kc[:, idxc]
        vg = vc[:, idxc]
        bias = rel_bias(table, j * dil)
        s = jnp.einsum('bthd,btjhd->bhtj', q, kg).astype(jnp.float32) * ATT_SCALE + bias[None, :, None, :]
        p, lse = masked_softmax_stats(s, valid[None, None])
        outs.append(jnp.einsum('bhtj,btjhd->bthd', p.astype(vc.dtype), vg))
        lses.append(lse.transpose(0, 2, 1))
    return combine_branches(outs, lses)

def mixer_inputs(h, w_in):
    N, T, _ = h.shape
    q, k, v, a, g = jnp.split(h @ w_in, [ATT_WIDTH, 2 * ATT_WIDTH, 3 * ATT_WIDTH,
                                         3 * ATT_WIDTH + CONV_WIDTH], axis=-1)
    shp = (N, T, N_ATT_HEADS, HEAD_DIM)
    u = a * jax.nn.sigmoid(g)
    return q.reshape(shp), k.reshape(shp), v.reshape(shp), u

def causal_dwconv(u_full, conv_w, conv_b):
    y = lax.conv_general_dilated(u_full, conv_w[:, None, :].astype(u_full.dtype), window_strides=(1,),
                                 padding='VALID', dimension_numbers=('NWC', 'WIO', 'NWC'),
                                 feature_group_count=CONV_WIDTH)
    return y + conv_b

def mixer_outputs(att, u_full, conv_w, conv_b, ln_g, ln_b, w_out):
    N, T = att.shape[:2]
    c = jax.nn.silu(layernorm(causal_dwconv(u_full, conv_w, conv_b), ln_g, ln_b))
    return jnp.concatenate([att.reshape(N, T, ATT_WIDTH), c], axis=-1) @ w_out

def mem_kv(mem, g, w_k, w_v):
    N, M, _ = mem.shape
    m = rmsnorm(mem, g)
    return ((m @ w_k).reshape(N, M, X_HEADS, X_HEAD_DIM),
            (m @ w_v).reshape(N, M, X_HEADS, X_HEAD_DIM))

def cross_attend(h, mk, mv, w_q, w_o):
    N, T, _ = h.shape
    q = (h @ w_q).reshape(N, T, X_HEADS, X_HEAD_DIM)
    s = jnp.einsum('bthd,bmhd->bhtm', q, mk).astype(jnp.float32) * X_SCALE
    p = jax.nn.softmax(s, axis=-1).astype(mv.dtype)
    o = jnp.einsum('bhtm,bmhd->bthd', p, mv).reshape(N, T, X_HEADS * X_HEAD_DIM)
    return o @ w_o

def swiglu(h, w_gate, w_up, w_down):
    return (jax.nn.silu(h @ w_gate) * (h @ w_up)) @ w_down

def setup_inputs(seed: int = 0) -> dict:
    key = jax.random.key(seed)
    ks = jax.random.split(key, 32)
    f32 = jnp.float32
    buf_len = min(MAX_WINDOW, PAST_LEN)

    def nrm(k, shape, scale=1.0):
        return jax.random.normal(k, shape, f32) * scale

    def gain(k, shape):
        return 1.0 + 0.05 * jax.random.normal(k, shape, f32)

    return {
        'x_prompt': nrm(ks[0], (BATCH, SEQ, D_MODEL)),
        'x_sample': nrm(ks[1], (DEC_BATCH, DEC_SEQ, D_MODEL)),
        'mem_prompt': nrm(ks[2], (BATCH, N_MEM, D_MODEL)),
        'cache_win_k': nrm(ks[3], (DEPTH, DEC_BATCH, buf_len, N_ATT_HEADS, HEAD_DIM)),
        'cache_win_v': nrm(ks[4], (DEPTH, DEC_BATCH, buf_len, N_ATT_HEADS, HEAD_DIM)),
        'cache_conv': nrm(ks[5], (DEPTH, DEC_BATCH, CONV_K - 1, CONV_WIDTH), 0.5),
        'cache_mem_k': nrm(ks[6], (DEPTH, DEC_BATCH, N_MEM, X_HEADS, X_HEAD_DIM)),
        'cache_mem_v': nrm(ks[7], (DEPTH, DEC_BATCH, N_MEM, X_HEADS, X_HEAD_DIM)),
        'rpb_table': nrm(ks[8], (N_BUCKETS, N_ATT_HEADS), 0.5),
        'norm_mix_g': gain(ks[9], (DEPTH, D_MODEL)),
        'w_in': nrm(ks[10], (DEPTH, D_MODEL, 3 * ATT_WIDTH + 2 * CONV_WIDTH), D_MODEL ** -0.5),
        'conv_w': nrm(ks[11], (DEPTH, CONV_K, CONV_WIDTH), CONV_K ** -0.5),
        'conv_b': nrm(ks[12], (DEPTH, CONV_WIDTH), 0.02),
        'conv_ln_g': gain(ks[13], (DEPTH, CONV_WIDTH)),
        'conv_ln_b': nrm(ks[14], (DEPTH, CONV_WIDTH), 0.02),
        'w_out': nrm(ks[15], (DEPTH, MIX_WIDTH, D_MODEL), MIX_WIDTH ** -0.5),
        'norm_x_g': gain(ks[16], (DEPTH, D_MODEL)),
        'norm_mem_g': gain(ks[17], (DEPTH, D_MODEL)),
        'w_xq': nrm(ks[18], (DEPTH, D_MODEL, X_HEADS * X_HEAD_DIM), D_MODEL ** -0.5),
        'w_xk': nrm(ks[19], (DEPTH, D_MODEL, X_HEADS * X_HEAD_DIM), D_MODEL ** -0.5),
        'w_xv': nrm(ks[20], (DEPTH, D_MODEL, X_HEADS * X_HEAD_DIM), D_MODEL ** -0.5),
        'w_xo': nrm(ks[21], (DEPTH, X_HEADS * X_HEAD_DIM, D_MODEL), (X_HEADS * X_HEAD_DIM) ** -0.5),
        'norm_ffn_g': gain(ks[22], (DEPTH, D_MODEL)),
        'w_ffn_gate': nrm(ks[23], (DEPTH, D_MODEL, D_FF), D_MODEL ** -0.5),
        'w_ffn_up': nrm(ks[24], (DEPTH, D_MODEL, D_FF), D_MODEL ** -0.5),
        'w_ffn_down': nrm(ks[25], (DEPTH, D_FF, D_MODEL), D_FF ** -0.5),
        'norm_final_g': gain(ks[26], (D_MODEL,)),
    }

def reference(x_prompt, x_sample, mem_prompt, cache_win_k, cache_win_v, cache_conv,
              cache_mem_k, cache_mem_v, rpb_table, norm_mix_g, w_in, conv_w, conv_b,
              conv_ln_g, conv_ln_b, w_out, norm_x_g, norm_mem_g, w_xq, w_xk, w_xv, w_xo,
              norm_ffn_g, w_ffn_gate, w_ffn_up, w_ffn_down, norm_final_g):
    buf_len = cache_win_k.shape[2]
    keep_p = min(MAX_WINDOW, x_prompt.shape[1])
    xp, xs = x_prompt, x_sample
    p_wk, p_wv, p_conv, p_mk, p_mv = [], [], [], [], []
    s_wk, s_wv, s_conv = [], [], []
    for l in range(DEPTH):
        q, k, v, u = mixer_inputs(rmsnorm(xp, norm_mix_g[l]), w_in[l])
        att = dilated_attention_prompt(q, k, v, rpb_table)
        u_full = jnp.pad(u, ((0, 0), (CONV_K - 1, 0), (0, 0)))
        xp = xp + mixer_outputs(att, u_full, conv_w[l], conv_b[l], conv_ln_g[l], conv_ln_b[l], w_out[l])
        p_wk.append(k[:, -keep_p:])
        p_wv.append(v[:, -keep_p:])
        p_conv.append(u_full[:, -(CONV_K - 1):])
        mk, mv = mem_kv(mem_prompt, norm_mem_g[l], w_xk[l], w_xv[l])
        p_mk.append(mk)
        p_mv.append(mv)
        xp = xp + cross_attend(rmsnorm(xp, norm_x_g[l]), mk, mv, w_xq[l], w_xo[l])
        xp = xp + swiglu(rmsnorm(xp, norm_ffn_g[l]), w_ffn_gate[l], w_ffn_up[l], w_ffn_down[l])

        q, k, v, u = mixer_inputs(rmsnorm(xs, norm_mix_g[l]), w_in[l])
        kc = jnp.concatenate([cache_win_k[l].astype(k.dtype), k], axis=1)
        vc = jnp.concatenate([cache_win_v[l].astype(v.dtype), v], axis=1)
        att = dilated_attention_sample(q, kc, vc, rpb_table, buf_len)
        u_full = jnp.concatenate([cache_conv[l].astype(u.dtype), u], axis=1)
        xs = xs + mixer_outputs(att, u_full, conv_w[l], conv_b[l], conv_ln_g[l], conv_ln_b[l], w_out[l])
        s_wk.append(kc[:, -buf_len:])
        s_wv.append(vc[:, -buf_len:])
        s_conv.append(u_full[:, -(CONV_K - 1):])
        xs = xs + cross_attend(rmsnorm(xs, norm_x_g[l]), cache_mem_k[l], cache_mem_v[l], w_xq[l], w_xo[l])
        xs = xs + swiglu(rmsnorm(xs, norm_ffn_g[l]), w_ffn_gate[l], w_ffn_up[l], w_ffn_down[l])

    y_prompt = rmsnorm(xp, norm_final_g)
    y_sample = rmsnorm(xs, norm_final_g)
    return (y_prompt, y_sample,
            jnp.stack(p_wk), jnp.stack(p_wv), jnp.stack(p_conv), jnp.stack(p_mk), jnp.stack(p_mv),
            jnp.stack(s_wk), jnp.stack(s_wv), jnp.stack(s_conv))


_drawn_inputs = setup_inputs


def setup_inputs(seed=0):
    import zlib

    import numpy as np

    out = dict(_drawn_inputs(seed))
    spreads = {}
    factors = {'conv_b': 4.631, 'conv_ln_g': 2.787, 'conv_ln_b': 8.0, 'norm_x_g': 8.0}
    for name, (base, spread) in spreads.items():
        noise = np.random.default_rng([zlib.crc32(name.encode()), seed]).standard_normal(out[name].shape)
        drawn = base * np.exp(spread * noise) if base else spread * noise
        out[name] = __import__('jax').numpy.asarray(drawn.astype(out[name].dtype))
    for name, factor in factors.items():
        out[name] = (out[name] * factor).astype(out[name].dtype)
    return out
```

```python
import math
from contextlib import ExitStack

import numpy as np

import concourse.bass as bass
from concourse import mybir

F32 = mybir.dt.float32
F32R = mybir.dt.float32r
ALU = mybir.AluOpType
ACT = mybir.ActivationFunctionType
AX = mybir.AxisListType

P = 128
D = 1024
KC = D // P
TP = 1024
NB, NI = 8, 8
TS = NB * NI
T = TP + TS
QT = TP // P
GROUPS = ((0, 364), (364, 362), (726, 362))
TOKEN_BANKS = ((0, 512), (512, 512), (1024, TS))
LAST_P = TP - GROUPS[2][0]
HD, NH = 64, 12
AW = HD * NH
CW = D - AW
PAIRS = NH // 2
TAPS, HIST = 31, 30
BUF = 2048
NM = 256
XH, XD = 4, 256
FF = 2816
FC = FF // P
EPS = 1e-6
MASKED = -1e30
LOWEST = -3e38

ZERO = 128
GL = ZERO + BUF + 16
STRIP = TP + P
FAR, NEAR = 6, 4
KT = FAR + NEAR
NEAR0 = BUF - NEAR * P
KEY_GROUPS = ((0, 4), (4, 8), (8, 10))
KEY_DMAS = (64, 48, 16)
FFT = FC // 2


def bucket_starts():
    def bucket(n):
        return n if n < 16 else min(31, 16 + int(math.log(n / 16) / math.log(128) * 16))
    return [next(n for n in range(BUF + 1) if bucket(n) >= b) for b in range(32)] + [BUF + 8]


def weight_turn(n, i=None, per=0):
    use = n // 2 + 1
    return n % 2, use if i is None else use + (per // 2) * i


class Pair:

    def __init__(self, c0, i=None):
        self.c0, self.i = c0, i
        self.slot = c0 % 2
        self.c = self.at(1, 0)

    def at(self, per_pair, count):
        fixed = per_pair * self.c0 + count
        return fixed if self.i is None else fixed + 2 * per_pair * self.i

    def first(self, per_pair, count):
        return per_pair * self.c0 + count <= 0

    def next(self):
        return Pair(self.c0 + 1, self.i)

    def weights(self, which):
        return weight_turn(FIRST_QKV + 3 * self.c0 + which, self.i, 6)


FIRST_QKV = 4


def layer_step(nc, A):
    ctx = ExitStack()
    with ctx:
        def sem(name):
            return ctx.enter_context(nc.semaphore(name))

        def sb(name, shape, dt=F32, where=ctx):
            return where.enter_context(nc.sbuf_tensor(name, shape, dt))

        bank = [ctx.enter_context(nc.psum_tensor(f"bank{i}", [P, 512], F32)) for i in range(8)]

        xT = sb("xT", [P, KC, T])
        w_raw = [sb(f"w_raw{i}", [P, 1024]) for i in range(2)]
        w_hi = [sb(f"w_hi{i}", [P, 1024], F32R) for i in range(2)]
        w_lo = [sb(f"w_lo{i}", [P, 1024], F32R) for i in range(2)]
        ident = sb("ident", [P, P])
        ones = sb("ones", [P, P])
        conv_vec = sb("conv_vec", [P, 2, 35])
        gains = sb("gains", [P, 24])
        eps = sb("eps", [P, 1])
        q_blk = sb("q_blk", [P, NB, PAIRS, 16])
        ks_T = sb("ks_T", [P, PAIRS, TS])
        ks_nat = sb("ks_nat", [TS, AW])
        vs_nat = sb("vs_nat", [TS, AW])
        y_conv = xT[:, PAIRS:KC, :]

        s1 = ExitStack()
        h_hi = sb("h_hi", [P, KC, T], F32R, s1)
        h_lo = sb("h_lo", [P, KC, T], F32R, s1)
        u_p = sb("u_p", [P, 2, HIST + TP + 1], where=s1)
        u_s = sb("u_s", [P, 2, NB, HIST + NI + 1], where=s1)
        s1a = ExitStack()
        x_work = sb("x_work", [P, 4, D], where=s1a)
        x_nat, x_sc = [x_work[:, i, :] for i in range(2)], [x_work[:, 2 + i, :] for i in range(2)]
        g_mix = sb("g_mix", [P, D], where=s1a)
        vec_nat = sb("vec_nat", [35, CW], where=s1a)
        gain_nat = sb("gain_nat", [24, P], where=s1a)
        cc_nat = sb("cc_nat", [120, 2, CW], where=s1a)
        ssq = sb("ssq", [P, 2], where=s1a)
        rms = sb("rms", [P, 2], where=s1a)
        rinv = sb("rinv", [P, 2], where=s1a)
        work = x_work[:, :, :].rearrange("p a c -> p (a c)")
        a_half, tanh_g = work[:, 0:T], work[:, T:2 * T]
        table = sb("table", [NH, 32], where=s1a)
        f_tab = sb("f_tab", [NH, BUF + 8], where=s1a)
        g_tab = sb("g_tab", [NH, GL], where=s1a)
        u_new = sb("u_new", [P, 2, TS], where=s1a)
        us_nat = sb("us_nat", [TS, CW], where=s1a)
        up_nat = sb("up_nat", [HIST, CW], where=s1a)
        s1a.close()
        q_T = [sb(f"q_T{i}", [P, TP], where=s1) for i in range(2)]
        k_T = [sb(f"k_T{i}", [P, T], where=s1) for i in range(2)]
        v_T = sb("v_T", [P, T], where=s1)
        v_nat = [sb(f"v_nat{i}", [P, QT, P], where=s1) for i in range(2)]
        k_nat = sb("k_nat", [P, QT, P], where=s1)
        strip = [sb(f"strip{i}", [P, STRIP], where=s1) for i in range(2)]
        sp = [sb(f"sp{i}", [P, TP], where=s1) for i in range(2)]
        p_T = sb("p_T", [P, TP], where=s1)
        att = sb("att", [P, QT, P], where=s1)
        smax = sb("smax", [P, 2, 2], where=s1)
        nmax = sb("nmax", [P, 2], where=s1)
        rsum = sb("rsum", [P, 2], where=s1)
        rrec = sb("rrec", [P, 2], where=s1)
        s1.close()

        s2 = ExitStack()
        kn = sb("kn", [P, KT, AW], where=s2)
        vn = [sb(f"vn{i}", [P, KT, AW], where=s2) for i in range(2)]
        kt = [sb(f"kt{i}", [P, 512], where=s2) for i in range(2)]
        q_pad = [sb(f"q_pad{i}", [P, PAIRS * 112], where=s2) for i in range(2)]
        srow = [sb(f"srow{i}", [96, KT * P + TS], where=s2) for i in range(2)]
        d_strip = sb("d_strip", [96, BUF + NI], where=s2)
        d_row = sb("d_row", [96, KT * P + TS], where=s2)
        d_new = sb("d_new", [96, 2 * 56 + NI], where=s2)
        pT_s = sb("pT_s", [P, KT + 1, 96], where=s2)
        o_sb = sb("o_sb", [96, AW], where=s2)
        smx = sb("smx", [96, 2, 8], where=s2)
        snm = sb("snm", [96, 2], where=s2)
        srs = sb("srs", [96, 2], where=s2)
        srr = sb("srr", [96, 2], where=s2)
        half_vec = sb("half_vec", [P, 2, 2], where=s2)
        ln_work = vn[1][:, :, :].rearrange("p a c -> p (a c)")
        ln_sq = ln_work[:, 0:2 * T].rearrange("p (c t) -> p c t", c=2)
        ln_sd = ln_work[:, 2 * T:3 * T]
        ln_th = ln_work[:, 3 * T:5 * T].rearrange("p (c t) -> p c t", c=2)
        s2.close()

        s3 = ExitStack()
        g_hi = sb("g_hi", [P, KC, T], F32R, s3)
        g_lo = sb("g_lo", [P, KC, T], F32R, s3)
        s3m = ExitStack()
        mk_T = sb("mk_T", [P, KC, NM], where=s3m)
        mv_nat = sb("mv_nat", [P, 2, D], where=s3m)
        s3a = ExitStack()
        def norm_tools(where, tag):
            return dict(sq=[sb(f"sq{i}{tag}", [P, T], where=where) for i in range(2)],
                        acc=sb(f"acc{tag}", [P, T], where=where),
                        tmp=[sb(f"tmp{i}{tag}", [P, T], where=where) for i in range(2)],
                        diag=sb(f"diag{tag}", [P, 9, P], where=where),
                        rms=sb(f"nrms{tag}", [P, 9], where=where),
                        rinv=sb(f"nrinv{tag}", [P, 9], where=where))
        tools_x = norm_tools(s3a, "x")
        mn = sb("mn", [P, 2, D], where=s3a)
        m_hi = sb("m_hi", [P, KC, NM], F32R, s3a)
        m_lo = sb("m_lo", [P, KC, NM], F32R, s3a)
        m_kv = [[sb(f"m_kv{i}{e}", [P, NM], where=s3a) for i in range(2)] for e in range(2)]
        mk_nat = tools_x["sq"][0][:, 0:2 * P].rearrange("p (t c) -> p t c", t=2)
        m_stat = sb("m_stat", [P, 6], where=s3a)
        m_ssq, m_rms, m_rinv = m_stat[:, 0:2], m_stat[:, 2:4], m_stat[:, 4:6]
        xr_slot = [mn[:, 0, :], mn[:, 1, :]] + [tools_x["sq"][i][:, 0:D] for i in range(2)] \
            + [tools_x["tmp"][0][:, 0:D], tools_x["acc"][:, 0:D]]
        s3a.close()
        s3b = ExitStack()
        qx_s = sb("qx_s", [P, KC, TS], where=s3b)
        s3c = ExitStack()
        qx = sb("qx", [P, KC, TP], where=s3c)
        xp = [sb(f"xp{i}", [P, NM], where=s3c) for i in range(2)]
        xp_T = [sb(f"xp_T{i}", [P, 2, 512], where=s3c) for i in range(2)]
        xmx = sb("xmx", [P, 2], where=s3c)
        xm = sb("xm", [P, 2], where=s3c)
        xrs = sb("xrs", [P, 2], where=s3c)
        xrr = sb("xrr", [P, 2], where=s3c)
        s3c.close()
        s3d = ExitStack()
        c_kv = [sb(f"c_kv{i}", [P, 2, D], where=s3d) for i in range(4)]
        ckt = [sb(f"ckt{i}", [P, 512], where=s3d) for i in range(2)]
        cq_pad = [sb(f"cq_pad{i}", [P, 320], where=s3d) for i in range(2)]
        cs = [sb(f"cs{i}", [P, NM], where=s3d) for i in range(2)]
        cp_T = [sb(f"cp_T{i}", [P, 2, P], where=s3d) for i in range(2)]
        c_out = [sb(f"c_out{i}", [P, D], where=s3d) for i in range(2)]
        c_stat = sb("c_stat", [P, 2, 4], where=s3d)
        s3d.close()
        s3b.close()
        s3m.close()
        s4 = ExitStack()
        tools_f = norm_tools(s4, "f")
        act_hi = sb("act_hi", [P, 2, T], F32R, s4)
        act_lo = sb("act_lo", [P, 2, T], F32R, s4)
        gated = sb("gated", [P, 2, T], where=s4)
        f_th = sb("f_th", [P, T], where=s4)
        s4.close()
        s3.close()
        s5 = ExitStack()
        y_nat = [sb(f"y_nat{i}", [P, D], where=s5) for i in range(QT + 1)]
        s5.close()

        N_OUT = FIRST_QKV + 3 * PAIRS
        N_MEM = N_OUT + KC
        N_XQ = N_MEM + 2 * KC
        N_XO = N_XQ + KC
        N_FFN = N_XO + KC
        N_SLICES = N_FFN + 6 * FFT
        w_loaded = [sem(f"w_loaded{i}") for i in range(2)]
        w_ready = [sem(f"w_ready{i}") for i in range(2)]
        w_hi_done = sem("w_hi_done")
        w_used = [sem(f"w_used{i}") for i in range(2)]
        vec_loaded = sem("vec_loaded")
        vec_turned = sem("vec_turned")
        tab_loaded = sem("tab_loaded")
        tab_step = sem("tab_step")
        tab_stored = sem("tab_stored")
        gmix_loaded = sem("gmix_loaded")
        x_loaded = [sem(f"x_loaded{i}") for i in range(2)]
        x_scaled = sem("x_scaled")
        x_rms = sem("x_rms")
        x_rinv = sem("x_rinv")
        x_turned = sem("x_turned")
        hi_done = sem("hi_done")
        lo_done = sem("lo_done")
        tick = sem("tick")
        pool_step = sem("pool_step")
        s1a_over = sem("s1a_over")
        glu_ready = sem("glu_ready")
        a_done = sem("a_done")
        t_done = sem("t_done")
        dve_step = sem("dve_step")
        u_done = sem("u_done")
        cc_loaded = sem("cc_loaded")
        un_done = sem("un_done")
        qkv_ready = sem("qkv_ready")
        qkv_done = sem("qkv_done")
        kv_turned = sem("kv_turned")
        kv_done = sem("kv_done")
        v_out = [sem(f"v_out{i}") for i in range(2)]
        k_out = sem("k_out")
        strip_loaded = [sem(f"strip_loaded{i}") for i in range(2)]
        sc_ready = [sem(f"sc_ready{i}") for i in range(2)]
        sc_free = [sem(f"sc_free{i}") for i in range(2)]
        nm_ready = sem("nm_ready")
        ex_done = sem("ex_done")
        p_turned = [sem(f"p_turned{i}") for i in range(2)]
        pt_done = [sem(f"pt_done{i}") for i in range(2)]
        pv_done = sem("pv_done")
        rr_done = sem("rr_done")
        norm_done = sem("norm_done")
        at_turned = sem("at_turned")
        at_done = sem("at_done")
        conv_done = sem("conv_done")
        stored = sem("stored")
        ln_sums = sem("ln_sums")
        ln_act = sem("ln_act")
        ln_step = sem("ln_step")
        strip_s = sem("strip_s")
        d_made = sem("d_made")
        qp_ready = sem("qp_ready")
        kn_in = [sem(f"kn_in{i}") for i in range(3)]
        vn_in = [sem(f"vn_in{i}") for i in range(2)]
        kt_turned = [sem(f"kt_turned{i}") for i in range(2)]
        kt_done = [sem(f"kt_done{i}") for i in range(2)]
        st_ready = sem("st_ready")
        sr_done = sem("sr_done")
        snm_done = sem("snm_done")
        sx_done = sem("sx_done")
        srr_done = sem("srr_done")
        spt_turned = [sem(f"spt_turned{i}") for i in range(3)]
        spt_done = [sem(f"spt_done{i}") for i in range(3)]
        ov_ready = sem("ov_ready")
        ov_done = [sem(f"ov_done{i}") for i in range(2)]
        so_ready = sem("so_ready")
        so_done = sem("so_done")
        xr_turned = sem("xr_turned")
        xr_done = [sem(f"xr_done{i}") for i in range(2)]

        r_ready = sem("r_ready")
        r_added = sem("r_added")
        r_squared = sem("r_squared")
        r_summed = sem("r_summed")
        n_sum = sem("n_sum")
        n_rms = sem("n_rms")
        n_rinv = sem("n_rinv")
        n_diag = sem("n_diag")
        n_bc = sem("n_bc")
        n_tmp = sem("n_tmp")
        n_hi = sem("n_hi")
        n_lo = sem("n_lo")
        m_in = sem("m_in")
        m_step = sem("m_step")
        m_turned = sem("m_turned")
        m_hi_done = sem("m_hi_done")
        m_lo_done = sem("m_lo_done")
        m_read = sem("m_read")
        mw_hi = sem("mw_hi")
        m_kv_turned = sem("m_kv_turned")
        m_kv_done = sem("m_kv_done")
        mk_out = sem("mk_out")
        xq_ready = sem("xq_ready")
        xq_done = sem("xq_done")
        xs_ready = sem("xs_ready")
        xmx_done = sem("xmx_done")
        xe_done = sem("xe_done")
        xn_done = sem("xn_done")
        xt_turned = sem("xt_turned")
        xt_done = sem("xt_done")
        xv_ready = sem("xv_ready")
        xv_hi = sem("xv_hi")
        xv_lo = sem("xv_lo")
        c_in = [sem(f"c_in{i}") for i in range(4)]
        cq_ready = sem("cq_ready")
        ct_turned = [sem(f"ct_turned{i}") for i in range(2)]
        ct_done = [sem(f"ct_done{i}") for i in range(2)]
        cs_ready = sem("cs_ready")
        c_act = sem("c_act")
        c_dve = sem("c_dve")
        c_turned = sem("c_turned")
        co_ready = sem("co_ready")
        co_done = [sem(f"co_done{i}") for i in range(2)]
        co_turned = sem("co_turned")
        co_hi = sem("co_hi")
        co_lo = sem("co_lo")
        c_zero = sem("c_zero")

        def own_head(h):
            return bank[h // 2][:, 256 * (h % 2):256 * (h % 2) + 256]\
                .rearrange("p (c b r) -> p c b r", c=2, b=4)[:, :, :, NI * h:NI * h + NI]
        f_ready = sem("f_ready")
        f_tanh = sem("f_tanh")
        f_gate = sem("f_gate")
        f_gated = sem("f_gated")
        f_hi = sem("f_hi")
        f_lo = sem("f_lo")
        d_ready = sem("d_ready")
        d_added = sem("d_added")
        y_scaled = sem("y_scaled")
        y_turned = sem("y_turned")
        y_done = [sem(f"y_done{i}") for i in range(2)]

        UNITS = [(hh, qb) for hh in range(2) for qb in range(QT)]
        SLOTS = len(UNITS) + 1

        def unit_keys(s):
            return (UNITS[s][1] + 1) * P

        def proj_products(slot, rhs_hi, rhs_lo, groups, banks, chunks=KC):
            out = []
            for g, (t0, n) in enumerate(groups):
                for kc in range(chunks):
                    for m, (w, r) in enumerate(((w_hi, rhs_hi), (w_hi, rhs_lo), (w_lo, rhs_hi))):
                        out.append((g, banks[g][:, 0:n], w[slot][:, kc * P:(kc + 1) * P],
                                    r[:, kc, t0:t0 + n], kc == 0 and m == 0,
                                    kc == chunks - 1 and m == 2))
            return out

        N_QKV = 9 * 3 * KC
        share = [(N_QKV * s // SLOTS, N_QKV * (s + 1) // SLOTS) for s in range(SLOTS)]
        ends_in = [[g for g in range(9) if a < 24 * (g + 1) <= b] for a, b in share]
        kv_slot = {}
        for which, last in ((0, 2), (1, 5)):
            s0 = next(s for s in range(SLOTS) if last in ends_in[s]) + 1
            for j in range(3):
                kv_slot[s0 + j] = 3 * which + j
        att_slot = {1: 0, 2: 1, 3: 2}
        assert not set(kv_slot) & set(att_slot)
        TURNS = ((0, 3), (3, 6), (6, 9))
        ATT_TURNS = ((0, 3), (3, 6), (6, 8))

        block = ctx.enter_context(nc.Block())

        @block.sync
        def _(sp_):
            def hold(s, value):
                sp_.wait_ge(s, value)
                sp_.sem_inc(tick, 1)

            def load_w(n, src):
                slot, use = weight_turn(n)
                if n >= 2:
                    sp_.wait_ge(w_ready[slot], use - 1)
                sp_.dma_start(w_raw[slot][:, :].rearrange("p (k c) -> p k c", c=P), src)\
                   .then_inc(w_loaded[slot], 16)

            def w_cols(w, c0):
                return w[:, c0:c0 + P].rearrange("(k p) c -> p k c", p=P)

            x_p, x_s = A["x_prompt"], A["x_sample"]
            sp_.dma_start(x_nat[0][:, :], x_p[0:P, :]).then_inc(x_loaded[0], 16)
            sp_.dma_start(g_mix[:, :], A["norm_mix_g"].partition_broadcast(P)).then_inc(gmix_loaded, 16)
            sp_.dma_start(x_nat[1][:, :], x_p[P:2 * P, :]).then_inc(x_loaded[1], 16)
            load_w(0, w_cols(A["w_in"], 3 * AW))
            load_w(1, w_cols(A["w_in"], 3 * AW + CW))
            sp_.dma_start(table[:, :], A["rpb_table"].rearrange("b h -> h b"),
                           allow_slow_non_contiguous=True).then_inc(tab_loaded, 16)
            sp_.wait_ge(pool_step, 4)
            sp_.dma_start(vec_nat[0:TAPS, :], A["conv_w"]).then_inc(vec_loaded, 16)
            for r, name in ((32, "conv_b"), (33, "conv_ln_g"), (34, "conv_ln_b")):
                sp_.dma_start(vec_nat[r:r + 1, :], A[name]).then_inc(vec_loaded, 16)
            for r, name in ((0, "norm_x_g"), (8, "norm_ffn_g"), (16, "norm_final_g")):
                sp_.dma_start(gain_nat[r:r + KC, :], A[name]).then_inc(vec_loaded, 16)
            for g in range(2):
                sp_.dma_start(cc_nat[:, g, :], A["cache_conv"][4 * g * HIST:(4 * g + 4) * HIST, :])\
                   .then_inc(cc_loaded, 16)
            for t in range(2, QT + 1):
                sp_.wait_ge(x_scaled, t - 1)
                if t < QT:
                    sp_.dma_start(x_nat[t % 2][:, :], x_p[t * P:(t + 1) * P, :])\
                       .then_inc(x_loaded[t % 2], 16)
                else:
                    sp_.dma_start(x_nat[t % 2][0:TS, :], x_s).then_inc(x_loaded[t % 2], 16)
            sp_.dma_start(A["out_conv_s"][:, 0:HIST - NI, :], A["cache_conv3"][:, NI:HIST, :])\
               .then_inc(stored, 16)
            sp_.wait_ge(tab_step, 24)
            sp_.dma_start(A["g_scratch"], g_tab[:, :]).then_inc(tab_stored, 16)
            load_w(2, w_cols(A["w_in"], 3 * AW + P))
            load_w(3, w_cols(A["w_in"], 3 * AW + CW + P))

            def load_strip(c, hh):
                head = 2 * c + hh
                if c:
                    sp_.wait_ge(nm_ready, 16 * (c - 1) + 8 * (hh + 1))
                sp_.dma_start(strip[hh][:, :], bass.AP(tensor=A["g_scratch"].tensor, offset=head * GL,
                                                       ap=[[1, P], [1, STRIP]])).then_inc(strip_loaded[hh], 16)

            def load_qkv(c, which):
                col = (2, 1, 0)[which] * AW + c * P
                load_w(FIRST_QKV + 3 * c + which, w_cols(A["w_in"], col))

            load_qkv(0, 0)
            sp_.wait_ge(tab_stored, 16)
            sp_.wait_ge(un_done, 2)
            sp_.wait_ge(u_done, 6)
            sp_.dma_start(A["out_conv_s"][:, HIST - NI:HIST, :], us_nat[:, :]).then_inc(stored, 16)
            sp_.dma_start(A["out_conv_p"], up_nat[:, :]).then_inc(stored, 16)
            load_qkv(0, 1)
            load_qkv(0, 2)
            sp_.wait_ge(stored, 48)
            sp_.sem_inc(s1a_over, 1)
            load_strip(0, 0)
            load_qkv(1, 0)
            for c in range(-1, PAIRS):
                if c >= 0:
                    load_strip(c, 1)
                if 0 <= c < PAIRS - 1:
                    load_qkv(c + 1, 1)
                    load_strip(c + 1, 0)
                    load_qkv(c + 1, 2)
                if c < PAIRS - 1:
                    n = c + 1
                    sp_.wait_ge(kv_done, 6 * n + 3)
                    sp_.dma_start(A["out_pv"].rearrange("(t p) c -> p t c", p=P)[:, :, n * P:(n + 1) * P],
                                  v_nat[n % 2][:, :, :]).then_inc(v_out[n % 2], 16)
                    if 0 <= c < PAIRS - 2:
                        load_qkv(c + 2, 0)
                    sp_.wait_ge(kv_done, 6 * n + 6)
                    sp_.dma_start(A["out_pk"].rearrange("(t p) c -> p t c", p=P)[:, :, n * P:(n + 1) * P],
                                  k_nat[:, :, :]).then_inc(k_out, 16)
            for b in range(NB):
                sp_.dma_start(A["out_sk"][b, BUF - NI:BUF, :], ks_nat[b * NI:(b + 1) * NI, :]).then_inc(stored, 16)
                sp_.dma_start(A["out_sv"][b, BUF - NI:BUF, :], vs_nat[b * NI:(b + 1) * NI, :]).then_inc(stored, 16)
            for c in range(2):
                load_w(N_OUT + c, w_cols(A["w_out"], c * P))
            ck_rows = A["cache_win_k"].rearrange("b t c -> (b t) c")
            cv_rows = A["cache_win_v"].rearrange("b t c -> (b t) c")

            def load_tiles(dst, src, row0, t0, t1, arrived):
                for t in range(t0, min(t1, FAR)):
                    part = src[bass.ds(row0 + 256 * t, 256), :].rearrange("(j r) c -> j r c", r=16)[:, 0:8, :]
                    sp_.dma_start(dst[:, t, :], part).then_inc(arrived, 16)
                near = max(t0, FAR)
                if t1 > near:
                    sp_.dma_start(dst[:, near:t1, :],
                                  src[bass.ds(row0 + NEAR0 + (near - FAR) * P, (t1 - near) * P), :]
                                  .rearrange("(t p) c -> p t c", p=P)).then_inc(arrived, 16)

            def load_batch(b, p):
                row0 = b * BUF
                for j, (t0, t1) in enumerate(KEY_GROUPS):
                    if not isinstance(b, int):
                        hold(kt_turned[1], 9 * b + (3 * j - 6))
                    elif b:
                        sp_.wait_ge(kt_turned[1], 3 * j + 3)
                    load_tiles(kn, ck_rows, row0, t0, t1, kn_in[j])
                if not isinstance(b, int):
                    hold(ov_ready, 2 * b - 2)
                elif b:
                    sp_.wait_ge(ln_step, 22)
                load_tiles(vn[p], cv_rows, row0, 0, KT, vn_in[p])

            slot, use = weight_turn(N_OUT - 1)
            sp_.wait_ge(w_used[slot], use)
            load_batch(0, 0)
            sp_.wait_ge(at_done, 18)
            sp_.wait_ge(conv_done, 2 + 32 * 4)
            sp_.wait_ge(v_out[0], 48)
            sp_.wait_ge(v_out[1], 48)
            sp_.wait_ge(k_out, 96)
            for h in range(NH):
                sp_.dma_start(d_strip[h * NI:(h + 1) * NI, :],
                              bass.AP(tensor=A["g_scratch"].tensor, offset=h * GL + ZERO - 7,
                                      ap=[[1, NI], [1, BUF + NI]])).then_inc(strip_s, 16)
            load_batch(1, 1)
            with sp_.Fori(0, NB // 2 - 1) as i:
                for p in range(2):
                    load_batch(2 * i + (2 + p), p)
            sp_.wait_ge(so_done, 4 * NB)
            sp_.dma_start(tools_x["tmp"][1][:, 0:D], A["norm_mem_g"].partition_broadcast(P)).then_inc(m_in, 16)
            for t in range(QT + 1):
                if t >= 6:
                    sp_.wait_ge(xr_turned, 2 * (t - 5))
                rows, src = (P, x_p[t * P:(t + 1) * P, :]) if t < QT else (TS, x_s)
                sp_.dma_start(xr_slot[t % 6][0:rows, :], src).then_inc(x_loaded[t // 3 % 2], 16)
            for t in range(2):
                sp_.wait_ge(xr_turned, 2 * (t + 7))
                sp_.dma_start(mn[:, t, :], A["mem_prompt"][t * P:(t + 1) * P, :]).then_inc(m_in, 16)

            def load_w_at(n, i, per, src):
                slot, use = weight_turn(n, i, per)
                hold(w_ready[slot], use - 1)
                sp_.dma_start(w_raw[slot][:, :].rearrange("p (k c) -> p k c", c=P), src)\
                   .then_inc(w_loaded[slot], 16)

            with sp_.Fori(1, KC // 2) as i:
                for c in range(2):
                    load_w_at(N_OUT + c, i, 2, A["w_out"][:, bass.ds((2 * i + c) * P, P)]
                              .rearrange("(k p) c -> p k c", p=P))
            def load_mem_w(i):
                for c, name in enumerate(("w_xk", "w_xv")):
                    load_w_at(N_MEM + c, i, 2, A[name][:, bass.ts(i, P)].rearrange("(k p) c -> p k c", p=P))

            for c, name in enumerate(("w_xk", "w_xv")):
                load_w(N_MEM + c, w_cols(A[name], 0))
            with sp_.Fori(1, KC) as i:
                load_mem_w(i)
            with sp_.Fori(0, KC // 2) as i:
                for c in range(2):
                    load_w_at(N_XQ + c, i, 2, A["w_xq"][:, bass.ds((2 * i + c) * P, P)]
                              .rearrange("(k p) c -> p k c", p=P))
            sp_.wait_ge(m_kv_done, 2 * KC + 2)
            sp_.dma_start(A["out_mv"].rearrange("(t p) c -> p t c", p=P), mv_nat[:, :, :]).then_inc(stored, 16)
            for c in range(2):
                load_w(N_XO + c, w_cols(A["w_xo"], c * P))
            for n in range(2 * NB):
                name, b = (("cache_mem_k", n) if n < NB else ("cache_mem_v", n - NB))
                if n < 4:
                    sp_.wait_ge(xs_ready, QT * (n + 1))
                elif n < NB + 4:
                    sp_.wait_ge(ct_turned[1], 2 * (n - 3))
                else:
                    sp_.wait_ge(co_ready, 2 * (n - NB - 3))
                sp_.dma_start(c_kv[n % 4][:, :, :], A[name][b, :, :].rearrange("(t p) c -> p t c", p=P))\
                   .then_inc(c_in[n % 4], 16)
            with sp_.Fori(1, KC // 2) as i:
                for c in range(2):
                    load_w_at(N_XO + c, i, 2, A["w_xo"][:, bass.ds((2 * i + c) * P, P)]
                              .rearrange("(k p) c -> p k c", p=P))
            def load_gate_up(n, i, row_i):
                for k, name in enumerate(("w_ffn_gate", "w_ffn_up") * 2):
                    if i is None:
                        load_w(n + k, w_cols(A[name], (k // 2) * P))
                    else:
                        load_w_at(n + k, i, 6, A[name][:, bass.ds((2 * i + (2 + k // 2)) * P, P)]
                                  .rearrange("(k p) c -> p k c", p=P))
                        copy_rows(i, k)

            def load_down(n, i):
                for k in range(2):
                    if i is None:
                        src = A["w_ffn_down"][(FC - 2) * P:FC * P, k * 512:(k + 1) * 512]
                        slot, use = weight_turn(n + k)
                        sp_.wait_ge(w_ready[slot], use - 1)
                    else:
                        src = A["w_ffn_down"][bass.ds(i * (2 * P), 2 * P), k * 512:(k + 1) * 512]
                        slot, use = weight_turn(n + k, i, 6)
                        hold(w_ready[slot], use - 1)
                    sp_.dma_start(w_raw[slot][:, :].rearrange("p (k c) -> p k c", c=512),
                                  src.rearrange("(k p) c -> p k c", p=P)).then_inc(w_loaded[slot], 16)
                    if i is not None:
                        copy_rows(i, 4 + k)

            third = (BUF - NI) // 3
            ok_rows = A["out_sk"].rearrange("b t c -> (b t) c")
            ov_rows = A["out_sv"].rearrange("b t c -> (b t) c")
            copying = [True]

            def copy_rows(i, k):
                if not copying[0]:
                    return
                src, dst = ((ck_rows, ok_rows), (cv_rows, ov_rows))[k // 3]
                row0 = i * BUF + (k % 3) * third
                sp_.dma_start(dst[bass.ds(row0, third), :], src[bass.ds(row0 + NI, third), :])\
                   .then_inc(stored, 16)

            load_gate_up(N_FFN, None, None)
            with sp_.Fori(0, NB) as i:
                load_gate_up(N_FFN + 4, i, None)
                load_down(N_FFN + 8, i)
            copying[0] = False
            with sp_.Fori(NB, FFT - 1) as i:
                load_gate_up(N_FFN + 4, i, None)
                load_down(N_FFN + 8, i)
            load_down(N_FFN + 6 * FFT - 2, None)
            for t in range(QT + 1):
                sp_.wait_ge(y_done[0], t + 1)
                sp_.wait_ge(y_done[1], t + 1)
                rows, dst = (P, A["out_yp"][t * P:(t + 1) * P, :]) if t < QT else (TS, A["out_ys"])
                sp_.dma_start(dst, y_nat[t][0:rows, :]).then_inc(stored, 16)
            sp_.wait_ge(mk_out, 16 * KC)
            sp_.wait_ge(v_out[0], 48)
            sp_.wait_ge(v_out[1], 48)
            sp_.wait_ge(k_out, 96)
            sp_.wait_ge(stored, 16 * (3 + 2 * NB + 1 + 6 * NB + QT + 1))

        @block.gpsimd
        def _(pool):
            pool.memset(ident[:, :], 0.0).then_inc(pool_step, 1)
            pool.memset(ones[:, :], 1.0).then_inc(pool_step, 1)
            pool.memset(eps[:, :], EPS).then_inc(pool_step, 1)
            pool.memset(vec_nat[:, :], 0.0).then_inc(pool_step, 1)
            pool.wait_ge(pool_step, 1)
            pool.affine_select(out=ident[:, :], in_=ident[:, :], compare_op=ALU.not_equal, fill=1.0, base=0,
                               pattern=[[-1, P]], channel_multiplier=1).then_inc(pool_step, 1)
            pool.memset(q_blk[:, :, :, :], 0.0).then_inc(pool_step, 1)

            def split(slot, use, first=False, behind=0):
                pool.wait_ge(w_loaded[slot], 16 * use)
                if not first:
                    pool.wait_ge(w_used[slot], use - 1)
                    pool.sem_inc(tick, 1)
                pool.tensor_copy(w_hi[slot][:, :], w_raw[slot][:, :]).then_inc(w_hi_done, 1)
                pool.wait_ge(w_hi_done, 2 * use + (slot - 1 - behind))
                pool.tensor_tensor(w_lo[slot][:, :], w_raw[slot][:, :], w_hi[slot][:, :].bitcast(F32),
                                   ALU.subtract).then_inc(w_ready[slot], 1)

            for slot in range(2):
                split(slot, 1, True)
            with pool.Fori(2, N_MEM // 2 + 1) as use:
                for slot in range(2):
                    split(slot, use)
            with pool.Fori(N_MEM // 2 + 1, N_XQ // 2 + 1) as use:
                for slot in range(2):
                    pool.wait_ge(mw_hi, 2 * use + (slot - 1 - N_MEM))
                    pool.tensor_tensor(w_lo[slot][:, :], w_raw[slot][:, :], w_hi[slot][:, :].bitcast(F32),
                                       ALU.subtract).then_inc(w_ready[slot], 1)
            with pool.Fori(N_XQ // 2 + 1, N_SLICES // 2 + 1) as use:
                for slot in range(2):
                    split(slot, use, behind=2 * KC)

        @block.tensor
        def _(pe):
            pe.wait_ge(pool_step, 5)
            pe.wait_ge(vec_loaded, 16 * 7)
            for c in range(2):
                pe.transpose(bank[7][:, 64 * c:64 * c + 35], vec_nat[:, c * P:(c + 1) * P], ident[0:35, 0:35])
            pe.transpose(bank[7][:, 128:152], gain_nat[:, :], ident[0:24, 0:24]).then_inc(vec_turned, 1)
            pe.wait_ge(cc_loaded, 32)
            for g in range(2):
                for c in range(2):
                    last = pe.transpose(bank[2][:, 120 * (2 * g + c):120 * (2 * g + c) + 120],
                                        cc_nat[:, g, c * P:(c + 1) * P], ident[0:120, 0:120])
            last.then_inc(vec_turned, 1)
            for t in range(QT + 1):
                rows = P if t < QT else TS
                pe.wait_ge(x_scaled, t + 1)
                for j in range(2):
                    if t >= 2:
                        pe.wait_ge(lo_done, 2 * (t - 2) + j + 1)
                    for i in range(4):
                        k = 4 * j + i
                        last = pe.transpose(bank[3 + 2 * (t % 2) + j][:, i * P:i * P + rows],
                                            x_sc[t % 2][0:rows, k * P:(k + 1) * P], ident[0:rows, 0:rows])
                    last.then_inc(x_turned, 1)
            for n in range(4):
                slot, use = weight_turn(n)
                pe.wait_ge(w_ready[slot], use)
                if n == 0:
                    pe.wait_ge(lo_done, 2 * (QT + 1))
                    pe.wait_ge(dve_step, 5)
                if n == 2:
                    pe.wait_ge(a_done, 3)
                if n == 3:
                    pe.wait_ge(t_done, 3)
                banks = bank[0:3] if n % 2 == 0 else bank[3:6]
                for g, out, w, r, start, stop in proj_products(slot, h_hi, h_lo, GROUPS, banks):
                    last = pe.matmul(out, w, r, start=start, stop=stop)
                    if stop and g < 2:
                        last.then_inc(glu_ready, 1)
                last.then_inc(w_used[slot], 1)

            def qkv_product(pair, m, products):
                which, at = divmod(m, 9 * KC)
                slot, use = pair.weights(which)
                g, out, w, r, start, stop = products[slot][at]
                if at == 0:
                    pe.wait_ge(w_ready[slot], use)
                if start and not pair.first(9, 3 * which + g - 2):
                    pe.wait_ge(qkv_done, pair.at(9, 3 * which + g - 2))
                last = pe.matmul(out, w, r, start=start, stop=stop)
                if stop and g < 2:
                    last.then_inc(qkv_ready, 1)
                elif stop:
                    last.then_inc(w_used[slot], 1)

            products = [proj_products(slot, h_hi, h_lo, GROUPS, bank[0:3]) for slot in range(2)]

            def turn_kv(pair, j):
                src, (t0, t1) = (v_T if j < 3 else k_T[pair.slot]), TURNS[j % 3]
                pe.wait_ge(qkv_done, pair.at(9, 3 if j < 3 else 6))
                if not pair.first(6, j):
                    pe.wait_ge(kv_done, pair.at(6, j))
                if not pair.first(3, -3):
                    pe.wait_ge(at_done, pair.at(3, -3))
                for t in range(t0, t1):
                    n = P if t < QT else TS
                    last = pe.transpose(bank[7][0:n, P * (1 + t - t0):P * (2 + t - t0)],
                                        src[:, t * P:t * P + n], ident[:, :])
                last.then_inc(kv_turned, 1)

            def turn_att(pair, j):
                t0, t1 = ATT_TURNS[j]
                pe.wait_ge(norm_done, pair.at(16, 16))
                pe.wait_ge(kv_done, min(36, 6 * (pair.c0 + 2)) if pair.i is None else pair.at(6, 12))
                if not pair.first(3, j):
                    pe.wait_ge(at_done, pair.at(3, j))
                for t in range(t0, t1):
                    last = pe.transpose(bank[7][:, P * (1 + t - t0):P * (2 + t - t0)], att[:, t, :], ident[:, :])
                last.then_inc(at_turned, 1)

            def scores(pair, s):
                hh, qb = UNITS[s]
                half = slice(HD * hh, HD * hh + HD)
                if s == 0:
                    pe.wait_ge(qkv_done, pair.at(9, 9))
                for j in range(1 + (qb >= 4)):
                    n = min(512, unit_keys(s) - 512 * j)
                    count = (16, s) if j == 0 else (8, 4 * hh + qb - 4)
                    if not pair.first(*count):
                        pe.wait_ge(sc_free[j], pair.at(*count))
                    pe.matmul(bank[3 + j][:, 0:n], q_T[pair.slot][half, qb * P:(qb + 1) * P],
                              k_T[pair.slot][half, 512 * j:512 * j + n], start=True, stop=True)\
                      .then_inc(sc_ready[j], 1)

            def turn_p(pair, s):
                pe.wait_ge(ex_done, pair.at(16, s + 1))
                for j in range(1 + (UNITS[s][1] >= 4)):
                    blocks = min(4, UNITS[s][1] + 1 - 4 * j)
                    for i in range(blocks):
                        last = pe.transpose(bank[5 + j][:, i * P:(i + 1) * P],
                                            sp[s % 2][:, (4 * j + i) * P:(4 * j + i + 1) * P], ident[:, :])
                    last.then_inc(p_turned[j], 1)

            def values(pair, s, before, ahead):
                hh, qb = UNITS[s]
                if s == 0:
                    pe.wait_ge(kv_done, pair.at(6, 6))
                if not pair.first(16, s):
                    pe.wait_ge(norm_done, pair.at(16, s))
                if before and s + 1 in att_slot:
                    pe.wait_ge(at_done, pair.at(3, att_slot[s + 1] - 2))
                if ahead and s + 1 in kv_slot:
                    pe.wait_ge(kv_done, pair.at(6, kv_slot[s + 1] + 7))
                for k in range(qb + 1):
                    if k % 4 == 0:
                        j = k // 4
                        pe.wait_ge(pt_done[j], pair.at(16, s + 1) if j == 0 else pair.at(8, 4 * hh + qb - 3))
                    last = pe.matmul(bank[7][:, HD * (s % 2):HD * (s % 2) + HD], p_T[:, k * P:(k + 1) * P],
                                     v_nat[pair.slot][:, k, HD * hh:HD * hh + HD], start=k == 0, stop=k == qb)
                last.then_inc(pv_done, 1)

            def attend(pair, before=True, ahead=True):
                after = pair.next()
                for s in range(SLOTS):
                    if s < 16:
                        scores(pair, s)
                    if s >= 1:
                        turn_p(pair, s - 1)
                    if s >= 2 and (before and s in att_slot or ahead and s in kv_slot):
                        pe.wait_ge(norm_done, pair.at(16, s - 1))
                    if before and s in att_slot:
                        turn_att(Pair(pair.c0 - 1, pair.i), att_slot[s])
                    if ahead and s in kv_slot:
                        turn_kv(after, kv_slot[s])
                    if ahead:
                        for m in range(*share[s]):
                            qkv_product(after, m, products)
                    if s >= 1:
                        values(pair, s - 1, before, ahead)

            pe.wait_ge(u_done, 6)
            for c in range(2):
                pe.transpose(bank[6][0:TS, c * P:(c + 1) * P], u_new[:, c, :], ident[:, :])
                last = pe.transpose(bank[6][0:HIST, CW + c * P:CW + (c + 1) * P], u_p[:, c, TP:TP + HIST],
                                    ident[:, :])
            last.then_inc(vec_turned, 1)
            for m in range(N_QKV):
                qkv_product(Pair(0), m, products)
                if m == 24 * 4:
                    for j in range(3):
                        turn_kv(Pair(0), j)
            for j in range(3, 6):
                turn_kv(Pair(0), j)
            pe.wait_ge(un_done, 2)
            attend(Pair(0), before=False)
            with pe.Fori(0, 2) as i:
                attend(Pair(1, i))
                attend(Pair(2, i))
            attend(Pair(5), ahead=False)
            for j in range(3):
                turn_att(Pair(5), j)
            pe.wait_ge(ln_step, 1)
            for g, (t0, n) in enumerate(GROUPS):
                for c in range(2):
                    last = pe.matmul(bank[g][:, 0:n], ones[:, :], y_conv[:, c, t0:t0 + n], start=c == 0, stop=c == 1)
                last.then_inc(ln_sums, 1)
            for g, (t0, n) in enumerate(GROUPS):
                pe.wait_ge(ln_act, 2)
                for c in range(2):
                    last = pe.matmul(bank[3 + g][:, 0:n], ones[:, :], ln_sq[:, c, t0:t0 + n],
                                     start=c == 0, stop=c == 1)
                last.then_inc(ln_sums, 1)

            pe.wait_ge(ln_step, 22)

            def b_at(b0, i, per, count):
                fixed = per * b0 + count
                return fixed if i is None else fixed + 2 * per * i

            def front(b0, i=None):
                p = b0 % 2
                for q in range(19):
                    if q < 18:
                        j, c = divmod(q, PAIRS)
                        t0, t1 = KEY_GROUPS[j]
                        if c == 0:
                            pe.wait_ge(kn_in[j], b_at(b0, i, KEY_DMAS[j], KEY_DMAS[j]))
                        if 9 * b0 + q // 2 > 0:
                            pe.wait_ge(kt_done[q % 2], b_at(b0, i, 9, q // 2))
                        for t in range(t0, t1):
                            last = pe.transpose(bank[q % 2][:, (t - t0) * P:(t - t0 + 1) * P],
                                                kn[:, t, c * P:(c + 1) * P], ident[:, :])
                        last.then_inc(kt_turned[q % 2], 1)
                    if q >= 1:
                        r = q - 1
                        j, c = divmod(r, PAIRS)
                        n = (KEY_GROUPS[j][1] - KEY_GROUPS[j][0]) * P
                        if c == 0:
                            if j == 0:
                                pe.wait_ge(qp_ready, b_at(b0, i, 1, 1))
                            if b0:
                                pe.wait_ge(sr_done, b_at(b0, i, 3, j - 2))
                            if j == 1 and b0 >= 2:
                                pe.wait_ge(so_done, b_at(b0, i, 4, -4))
                        pe.wait_ge(kt_done[r % 2], b_at(b0, i, 9, r // 2 + 1))
                        last = pe.matmul(bank[2 + j][0:96, 0:n], q_pad[p][:, 96 * c:96 * c + 96], kt[r % 2][:, 0:n],
                                         start=c == 0, stop=c == PAIRS - 1)
                        if c == PAIRS - 1:
                            if j == 2:
                                for c in range(PAIRS):
                                    last = pe.matmul(bank[4][0:96, n:n + TS], q_pad[p][:, 96 * c:96 * c + 96],
                                                     ks_T[:, c, :], start=c == 0, stop=c == PAIRS - 1)
                            last.then_inc(st_ready, 1)
                    if q == 3 and b0 >= 2:
                        turn_out(b0 - 2, i)

            def turn_out(b0, i=None):
                for e in range(2):
                    pe.wait_ge(ov_done[e], b_at(b0, i, 1, 1))
                for e in range(2):
                    for c in range(3):
                        last = pe.transpose(bank[(7, 3)[e]][:, 96 * c:96 * c + 96],
                                            o_sb[:, (3 * e + c) * P:(3 * e + c + 1) * P], ident[0:96, 0:96])
                    last.then_inc(so_ready, 1)

            def back(b0, i=None, alone=False):
                p = b0 % 2
                pe.wait_ge(sx_done, b_at(b0, i, 1, 1))
                for j, (t0, t1) in enumerate(((0, 5), (5, 10), (10, 11))):
                    if j == 0 and b0 > 0:
                        pe.wait_ge(so_done, b_at(b0, i, 4, 0))
                    if j and not alone:
                        pe.wait_ge(sr_done, b_at(b0, i, 3, 3 + j))
                        if j == 2:
                            pe.sem_inc(tick, 1)
                    for t in range(t0, t1):
                        n = P if t < KT else TS
                        last = pe.transpose(bank[(7, 2, 3)[j]][0:n, 96 * (t - t0):96 * (t - t0) + 96],
                                            srow[p][:, t * P:t * P + n], ident[0:96, 0:96])
                    last.then_inc(spt_turned[j], 1)
                pe.wait_ge(vn_in[p], b_at(b0 // 2 * 2, i, 56, 112))
                for j in range(3):
                    pe.wait_ge(spt_done[j], b_at(b0, i, 1, 1))
                for e in range(2):
                    if b0:
                        pe.wait_ge(ov_done[e], b_at(b0, i, 1, 0))
                    out, cols = bank[5 + e][0:96, 0:AW // 2], slice(e * AW // 2, (e + 1) * AW // 2)
                    for t in range(KT):
                        pe.matmul(out, pT_s[:, t, :], vn[p][:, t, cols], start=t == 0, stop=False)
                    pe.matmul(out, pT_s[0:TS, KT, :], vs_nat[:, cols], start=False, stop=True).then_inc(ov_ready, 1)

            front(0)
            front(1)
            back(0)
            with pe.Fori(0, NB // 2 - 1) as i:
                front(2, i)
                back(1, i)
                front(3, i)
                back(2, i)
            turn_out(NB - 2)
            back(NB - 1, alone=True)
            turn_out(NB - 1)

            pe.wait_ge(so_done, 4 * NB)
            for t in range(QT + 1):
                rows = P if t < QT else TS
                if t % 3 == 0:
                    pe.wait_ge(x_loaded[t // 3 % 2], (16 * 8, 16 * 7, 16 * 11)[t // 3])
                for j in range(2):
                    if t >= 2:
                        pe.wait_ge(xr_done[j], t - 1)
                    for k in range(4):
                        last = pe.transpose(bank[3 + 2 * (t % 2) + j][:, k * P:k * P + rows],
                                            xr_slot[t % 6][0:rows, (4 * j + k) * P:(4 * j + k + 1) * P],
                                            ident[0:rows, 0:rows])
                    last.then_inc(xr_turned, 1)

            def project_stream(n0, turns, step, rhs, banks, groups, free, ready, free_per, base=0):
                prods = [proj_products(s, *rhs, groups, banks[s]) for s in range(2)]
                ng = len(groups)
                with pe.Fori(0, turns) as i:
                    for s in range(2):
                        slot, use = weight_turn(n0 + s, i, 2)
                        pe.wait_ge(w_ready[slot], use)
                        for g, out, w, r, start, stop in prods[s]:
                            if start:
                                pe.wait_ge(free, free_per * i + (base + s * (free_per // 2) + (g if ng > 1 else 0) + 1))
                            last = pe.matmul(out, w, r, start=start, stop=stop)
                            if stop and g < ng - 1:
                                last.then_inc(ready, 1)
                        last.then_inc(w_used[slot], 1)
                        if step:
                            step(i, s)

            def norm_sums(tools, turn):
                pe.wait_ge(r_summed, (KC + 1) * (turn + 1))
                for t in range(QT + 1):
                    n = P if t < QT else TS
                    last = pe.matmul(bank[7][0:n, t:t + 1], tools["acc"][:, t * P:t * P + n], ones[:, 0:1],
                                     start=True, stop=True)
                last.then_inc(n_sum, 1)

            def norm_factors(tools, turn):
                for t in range(QT + 1):
                    n = P if t < QT else TS
                    pe.wait_ge(n_diag, (QT + 1) * turn + t + 1)
                    last = pe.matmul(bank[3 + t // 4][:, (t % 4) * P:(t % 4) * P + n], ones[0:n, :],
                                     tools["diag"][0:n, t, 0:n], start=True, stop=True)
                    if t % 4 == 3 or t == QT:
                        last.then_inc(n_bc, 1)

            residual_banks = [bank[0:3], bank[3:6]]
            pe.wait_ge(xr_done[0], QT + 1)
            pe.wait_ge(xr_done[1], QT + 1)
            project_stream(N_OUT, KC // 2, None, (g_hi, g_lo), residual_banks, GROUPS,
                           r_added, r_ready, 6)
            mem_banks = (bank[0], bank[1], bank[2], bank[6])
            pe.wait_ge(r_added, 30)
            for t in range(2):
                pe.wait_ge(m_step, 6 + t)
                for j in range(2):
                    for k in range(4):
                        last = pe.transpose(mem_banks[2 * t + j][:, k * P:(k + 1) * P],
                                            mn[:, t, (4 * j + k) * P:(4 * j + k + 1) * P], ident[:, :])
                    last.then_inc(m_turned, 1)
            norm_sums(tools_x, 0)

            mem_prods = [proj_products(s, m_hi, m_lo, ((0, NM),), [bank[s]]) for s in range(2)]

            def mem_slice(c, kv):
                slot, use = weight_turn(N_MEM + 2 * c + kv)
                pe.wait_ge(w_ready[slot], use)
                if c:
                    pe.wait_ge(m_read, 2 * (c - 1) + kv + 1)
                for _, out, w, r, start, stop in mem_prods[kv]:
                    last = pe.matmul(out, w, r, start=start, stop=stop)
                last.then_inc(w_used[slot], 1)

            def turn_mem(c):
                for kv in range(2):
                    pe.wait_ge(m_read, 2 * c + kv + 1)
                    pe.wait_ge(m_kv_done, 2 * c + kv + 1)
                    for t in range(2):
                        last = pe.transpose((bank[2], bank[6])[kv][:, t * P:(t + 1) * P],
                                            m_kv[c % 2][kv][:, t * P:(t + 1) * P], ident[:, :])
                    last.then_inc(m_kv_turned, 1)

            pe.wait_ge(m_lo_done, 4)
            mem_slice(0, 0)
            mem_slice(0, 1)
            norm_factors(tools_x, 0)
            for c in range(1, KC):
                mem_slice(c, 0)
                turn_mem(c - 1)
                mem_slice(c, 1)
            turn_mem(KC - 1)
            pe.wait_ge(n_lo, 2 * KC)
            pe.wait_ge(m_kv_done, 2 * KC + 2)
            project_stream(N_XQ, KC // 2, None, (g_hi, g_lo), residual_banks, GROUPS, xq_done, xq_ready, 6)
            pe.wait_ge(xq_done, 6 + 3 * KC)
            XU = XH * QT
            for v in range(XU + 3):
                if v < XU:
                    h, qb = divmod(v, QT)
                    if v >= 2:
                        pe.wait_ge(xe_done, v - 1)
                    for c in range(2):
                        last = pe.matmul(bank[v % 2][:, 0:NM], qx[:, 2 * h + c, qb * P:(qb + 1) * P],
                                         mk_T[:, 2 * h + c, :], start=c == 0, stop=c == 1)
                    last.then_inc(xs_ready, 1)
                if 2 <= v < XU + 2:
                    u = v - 2
                    pe.wait_ge(xn_done, 2 * u + 2)
                    if u >= 2:
                        pe.wait_ge(xt_done, u - 1)
                    for m in range(2):
                        last = pe.transpose(bank[2 + u % 2][:, m * P:(m + 1) * P], xp[u % 2][:, m * P:(m + 1) * P],
                                            ident[:, :])
                    last.then_inc(xt_turned, 1)
                if v >= 3 and (v - 3) % 4 == 3:
                    u = v - 3
                    hf = u // 4
                    h = hf // 2
                    pe.wait_ge(xt_done, u + 1)
                    for c in range(2):
                        if hf >= 2:
                            pe.wait_ge(xv_lo, 2 * (hf - 2) + c + 1)
                        for m in range(2):
                            last = pe.matmul(bank[4 + 2 * (hf % 2) + c][:, :],
                                             mv_nat[:, m, h * XD + c * P:h * XD + (c + 1) * P],
                                             xp_T[hf % 2][:, m, :], start=m == 0, stop=m == 1)
                        last.then_inc(xv_ready, 1)
            pe.wait_ge(xv_lo, 16)
            for q in range(XH * NB + 1):
                if q < XH * NB:
                    b, h = divmod(q, XH)
                    if h == 0:
                        pe.wait_ge(c_in[b % 4], 16 * (b // 4 + 1))
                    if q >= 2:
                        pe.wait_ge(ct_done[q % 2], q // 2)
                    for c in range(2):
                        for m in range(2):
                            last = pe.transpose(bank[q % 2][:, (2 * c + m) * P:(2 * c + m + 1) * P],
                                                c_kv[b % 4][:, m, (2 * h + c) * P:(2 * h + c + 1) * P], ident[:, :])
                    last.then_inc(ct_turned[q % 2], 1)
                if q >= 1:
                    b, h = divmod(q - 1, XH)
                    if h == 0:
                        pe.wait_ge(cq_ready, b + 1)
                    pe.wait_ge(ct_done[(q - 1) % 2], (q - 1) // 2 + 1)
                    for c in range(2):
                        last = pe.matmul(bank[4 + b // 4][32 * (b % 4):32 * (b % 4) + 32, 0:NM],
                                         cq_pad[b % 2][:, 32 * (2 * h + c):32 * (2 * h + c) + 32],
                                         ckt[(q - 1) % 2][:, c * NM:(c + 1) * NM], start=h == 0 and c == 0,
                                         stop=h == XH - 1 and c == 1)
                    if h == XH - 1:
                        last.then_inc(cs_ready, 1)
            for e in range(2):
                pe.wait_ge(c_act, 2 * e + 1)
                for m in range(2):
                    last = pe.transpose(bank[2 + e][:, m * P:(m + 1) * P], cs[e][:, m * P:(m + 1) * P], ident[:, :])
                last.then_inc(c_turned, 1)
                pe.wait_ge(c_act, 2 * e + 2)
                for b4 in range(4):
                    b = 4 * e + b4
                    pe.wait_ge(c_in[b % 4], 16 * (b // 4 + 3))
                    for half in range(2):
                        if e and b4 == 0:
                            pe.wait_ge(co_done[half], 1)
                        for m in range(2):
                            last = pe.matmul(bank[6 + half][32 * b4:32 * b4 + 32, :],
                                             cp_T[e][:, m, 32 * b4:32 * b4 + 32],
                                             c_kv[b % 4][:, m, 512 * half:512 * half + 512],
                                             start=m == 0, stop=m == 1)
                        last.then_inc(co_ready, 1)
            for e in range(2):
                for half in range(2):
                    pe.wait_ge(co_done[half], e + 1)
                    if e:
                        pe.wait_ge(co_lo, 2 * half + 2)
                    for k in range(4):
                        last = pe.transpose(bank[half][:, k * P:(k + 1) * P],
                                            c_out[e][:, (4 * half + k) * P:(4 * half + k + 1) * P], ident[:, :])
                    last.then_inc(co_turned, 1)
            pe.wait_ge(co_lo, 8)
            project_stream(N_XO, KC // 2, None, (g_hi, g_lo), residual_banks, GROUPS,
                           r_added, r_ready, 6, 30)
            norm_sums(tools_f, 1)
            norm_factors(tools_f, 1)
            pe.wait_ge(n_lo, 3 * KC)

            ffn_prods = [[proj_products(s, g_hi, g_lo, GROUPS, bank[3 * s:3 * s + 3]) for s in range(2)]]

            def gate_up(n, i=None):
                for k in range(4):
                    slot, use = weight_turn(n + k, i, 6)
                    pe.wait_ge(w_ready[slot], use)
                    first_ch = 0 if i is None else 2
                    for g, out, w, r, start, stop in ffn_prods[0][k % 2]:
                        ev = 3 * (first_ch + k // 2 - 1) + g + 1
                        if start and ev > 0:
                            pe.wait_ge(f_gate if k % 2 == 0 else f_gated, ev if i is None else 6 * i + ev)
                        last = pe.matmul(out, w, r, start=start, stop=stop)
                        if stop and g < 2:
                            last.then_inc(f_ready, 1)
                    last.then_inc(w_used[slot], 1)

            def down(n, i=None):
                r_of = lambda r: (24 * (FFT - 1) + r) if i is None else 24 * i + r
                pe.wait_ge(f_lo, 2 * FFT if i is None else 2 * i + 2)
                for k in range(2):
                    slot, use = weight_turn(n + k, i, 6)
                    pe.wait_ge(w_ready[slot], use)
                    for o in range(4):
                        for g, (t0, w) in enumerate(GROUPS):
                            r = 3 * (4 * k + o) + g
                            pe.wait_ge(d_added, r_of(r + 1))
                            for j in range(2):
                                for m, (wt, rhs) in enumerate(((w_hi, act_hi), (w_hi, act_lo), (w_lo, act_hi))):
                                    last = pe.matmul(bank[6 + r % 2][:, 0:w],
                                                     wt[slot][:, j * 512 + o * P:j * 512 + (o + 1) * P],
                                                     rhs[:, j, t0:t0 + w], start=j == 0 and m == 0,
                                                     stop=j == 1 and m == 2)
                            if o == 3 and g == 2:
                                last.then_inc(w_used[slot], 1)
                            else:
                                last.then_inc(d_ready, 1)

            gate_up(N_FFN)
            with pe.Fori(0, FFT - 1) as i:
                gate_up(N_FFN + 4, i)
                down(N_FFN + 8, i)
            down(N_FFN + 6 * FFT - 2)
            pe.wait_ge(d_added, 24 * FFT + 2)
            norm_sums(tools_f, 2)
            pe.wait_ge(y_scaled, KC)
            for t in range(QT + 1):
                n = P if t < QT else TS
                for j in range(2):
                    if t >= 2:
                        pe.wait_ge(y_done[j], t - 1)
                    for k in range(4):
                        last = pe.transpose(mem_banks[2 * (t % 2) + j][0:n, k * P:(k + 1) * P],
                                            xT[:, 4 * j + k, t * P:t * P + n], ident[:, :])
                    last.then_inc(y_turned, 1)

        @block.scalar
        def _(act):
            act.wait_ge(pool_step, 5)
            for t in range(QT + 1):
                p, rows = t % 2, (P if t < QT else TS)
                act.wait_ge(x_loaded[p], 16 * (t // 2 + 1))
                if t >= 2:
                    act.wait_ge(x_turned, 2 * (t - 1))
                act.activation(x_sc[p][0:rows, :], x_nat[p][0:rows, :], ACT.Square,
                               accum_out=ssq[0:rows, p:p + 1]).then_inc(x_rms, 1)
                act.wait_ge(x_rms, 2 * t + 1)
                act.activation(rms[0:rows, p:p + 1], ssq[0:rows, p:p + 1], ACT.Sqrt, bias=eps[0:rows, 0:1],
                               scale=1.0 / D).then_inc(x_rms, 1)
                for tt in ([t - 1] if t else []) + ([t] if t == QT else []):
                    n = P if tt < QT else TS
                    for j in range(2):
                        act.wait_ge(x_turned, 2 * tt + j + 1)
                        src = bank[3 + 2 * (tt % 2) + j][:, :].rearrange("p (k n) -> p k n", k=4)[:, :, 0:n]
                        act.activation(h_hi[:, 4 * j:4 * j + 4, tt * P:tt * P + n], src, ACT.Copy)\
                           .then_inc(hi_done, 1)
            for n in range(4):
                slot, use = weight_turn(n)
                for g, (t0, w) in enumerate(GROUPS):
                    if g < 2:
                        act.wait_ge(glu_ready, 2 * n + g + 1)
                    else:
                        act.wait_ge(w_used[slot], use)
                    if n >= 2:
                        act.wait_ge(u_done, g + 1)
                    if n % 2 == 0:
                        act.activation(a_half[:, t0:t0 + w], bank[g][:, 0:w], ACT.Copy, scale=0.5)\
                           .then_inc(a_done, 1)
                    else:
                        act.activation(tanh_g[:, t0:t0 + w], bank[3 + g][:, 0:w], ACT.Tanh, scale=0.5)\
                           .then_inc(t_done, 1)
            act.wait_ge(vec_turned, 3)
            act.activation(us_nat[:, :], bank[6][0:TS, 0:CW], ACT.Copy).then_inc(un_done, 1)
            act.activation(up_nat[:, :], bank[6][0:HIST, CW:2 * CW], ACT.Copy).then_inc(un_done, 1)
            act.wait_ge(s1a_over, 1)

            def attend(pair):
                for s in range(SLOTS):
                    if s >= 1:
                        u = s - 1
                        hh, qb = UNITS[u]
                        for j in range(1 + (qb >= 4)):
                            n = min(512, unit_keys(u) - 512 * j)
                            act.wait_ge(p_turned[j], pair.at(16, u + 1) if j == 0 else pair.at(8, 4 * hh + qb - 3))
                            if j == 0 and not pair.first(16, u):
                                act.wait_ge(pv_done, pair.at(16, u))
                            act.activation(p_T[:, 512 * j:512 * j + n], bank[5 + j][:, 0:n], ACT.Copy)\
                               .then_inc(pt_done[j], 1)
                    if s < 16:
                        act.wait_ge(nm_ready, pair.at(16, s + 1))
                        if not pair.first(16, s - 1):
                            act.wait_ge(norm_done, pair.at(16, s - 1))
                        n = unit_keys(s)
                        act.activation(sp[s % 2][:, 0:n], sp[s % 2][:, 0:n], ACT.Exp,
                                       bias=nmax[:, s % 2:s % 2 + 1],
                                       accum_out=rsum[:, s % 2:s % 2 + 1]).then_inc(ex_done, 1)

            attend(Pair(0))
            with act.Fori(0, 2) as i:
                attend(Pair(1, i))
                attend(Pair(2, i))
            attend(Pair(5))
            for c in range(2):
                act.wait_ge(ln_step, 1 + 3 * (c + 1))
                act.activation(ln_sq[:, c, :], y_conv[:, c, :], ACT.Square).then_inc(ln_act, 1)
            for g, (t0, n) in enumerate(GROUPS):
                act.wait_ge(ln_sums, 3 + g + 1)
                act.activation(ln_sd[:, t0:t0 + n], bank[3 + g][:, 0:n], ACT.Sqrt, bias=eps[:, 0:1],
                               scale=1.0 / CW).then_inc(ln_act, 1)
            for c in range(2):
                for g, (t0, n) in enumerate(GROUPS):
                    act.wait_ge(ln_step, 10 + 3 * c + g + 1)
                    act.activation(ln_sq[:, c, t0:t0 + n], y_conv[:, c, t0:t0 + n], ACT.Identity,
                                   bias=half_vec[:, c, 1:2], scale=half_vec[:, c, 0:1]).then_inc(ln_act, 1)
                    act.wait_ge(ln_act, 5 + 2 * (3 * c + g) + 1)
                    act.activation(ln_th[:, c, t0:t0 + n], ln_sq[:, c, t0:t0 + n], ACT.Tanh).then_inc(ln_act, 1)

            def s_at(b0, i, per, count):
                fixed = per * b0 + count
                return fixed if i is None else fixed + 2 * per * i

            def front(b0, i=None):
                for q in range(0, 18, 2):
                    n = 512 if q < 12 else 256
                    act.wait_ge(kt_turned[0], s_at(b0, i, 9, q // 2 + 1))
                    act.activation(kt[0][:, 0:n], bank[0][:, 0:n], ACT.Copy).then_inc(kt_done[0], 1)

            def softmax(b0, i=None):
                p = b0 % 2
                act.wait_ge(snm_done, s_at(b0, i, 2, 2))
                act.activation(srow[p][:, :], srow[p][:, :], ACT.Exp, bias=snm[:, p:p + 1],
                               accum_out=srs[:, p:p + 1]).then_inc(sx_done, 1)

            def turned_probs(b0, i=None):
                act.wait_ge(spt_turned[0], s_at(b0, i, 1, 1))
                act.activation(pT_s[:, 0:5, :], bank[7][:, 0:480].rearrange("p (k n) -> p k n", k=5), ACT.Copy)\
                   .then_inc(spt_done[0], 1)
                act.wait_ge(spt_turned[2], s_at(b0, i, 1, 1))
                act.activation(pT_s[0:TS, KT, :], bank[3][0:TS, 0:96], ACT.Copy).then_inc(spt_done[2], 1)

            def scale_out(b0, i=None):
                p = b0 % 2
                act.wait_ge(srr_done, s_at(b0, i, 1, 1))
                act.wait_ge(ov_ready, s_at(b0, i, 2, 1))
                act.activation(o_sb[:, 0:AW // 2], bank[5][0:96, 0:AW // 2], ACT.Copy, scale=srr[:, p:p + 1])\
                   .then_inc(ov_done[0], 1)

            front(0)
            softmax(0)
            front(1)
            turned_probs(0)
            softmax(1)
            scale_out(0)
            with act.Fori(0, NB // 2 - 1) as i:
                for b0 in (2, 3):
                    front(b0, i)
                    turned_probs(b0 - 1, i)
                    softmax(b0, i)
                    scale_out(b0 - 1, i)
            turned_probs(NB - 1)
            scale_out(NB - 1)
            act.wait_ge(so_done, 4 * NB)
            for k in range(KC):
                act.activation(g_hi[:, k, :], xT[:, k, :], ACT.Copy).then_inc(n_hi, 1)
            act.wait_ge(n_lo, KC)
            for t in range(QT + 1):
                n = P if t < QT else TS
                act.wait_ge(xr_turned, 2 * t + 1)
                act.activation(xT[:, 0:4, t * P:t * P + n],
                               bank[3 + 2 * (t % 2)][:, :].rearrange("p (k n) -> p k n", k=4)[:, :, 0:n],
                               ACT.Copy).then_inc(xr_done[0], 1)

            act.wait_ge(m_in, 48)
            for t in range(2):
                if t:
                    act.wait_ge(m_step, 2 * t)
                act.activation(tools_x["tmp"][0][:, 0:D], mn[:, t, :], ACT.Square,
                               accum_out=m_ssq[:, t:t + 1]).then_inc(m_step, 1)
                act.wait_ge(m_step, 2 * t + 1)
                act.activation(m_rms[:, t:t + 1], m_ssq[:, t:t + 1], ACT.Sqrt, bias=eps[:, 0:1], scale=1.0 / D)\
                   .then_inc(m_step, 1)

            def squares(tools, turn):
                with act.Fori(0, KC // 2) as i:
                    for s in range(2):
                        act.wait_ge(r_added, 6 * i + (30 * turn + 6 + 3 * s + 3))
                        act.sem_inc(tick, 1)
                        act.activation(tools["sq"][s][:, :], xT[:, 2 * i + s, :], ACT.Square)\
                           .then_inc(r_squared, 1)

            def root(tools, turn):
                act.wait_ge(n_sum, turn + 1)
                for a, z, n in ((0, QT, P), (QT, QT + 1, TS)):
                    act.activation(tools["rms"][0:n, a:z], bank[7][0:n, a:z], ACT.Sqrt, bias=eps[0:n, 0:1],
                                   scale=1.0 / D).then_inc(n_rms, 1)

            def hi_part(tools, turn, k):
                    act.wait_ge(n_tmp, 3 * (KC * turn + k + 1))
                    act.activation(g_hi[:, k, :], tools["tmp"][k % 2][:, :], ACT.Copy).then_inc(n_hi, 1)

            squares(tools_x, 0)
            for t in range(2):
                for j in range(2):
                    act.wait_ge(m_turned, 2 * t + j + 1)
                    act.activation(m_hi[:, 4 * j:4 * j + 4, t * P:(t + 1) * P],
                                   (bank[0], bank[1], bank[2], bank[6])[2 * t + j][:, :]
                                   .rearrange("p (k n) -> p k n", k=4), ACT.Copy).then_inc(m_hi_done, 1)

            def mem_w_hi(n):
                slot, use = weight_turn(n)
                act.wait_ge(w_loaded[slot], 16 * use)
                act.wait_ge(w_used[slot], use - 1)
                act.activation(w_hi[slot][:, :], w_raw[slot][:, :], ACT.Copy).then_inc(mw_hi, 1)

            def store_keys(c):
                act.wait_ge(m_kv_done, 2 * c + 3)
                act.dma_start(A["out_mk"].rearrange("(t p) c -> p t c", p=P)[:, :, c * P:(c + 1) * P], mk_nat)\
                   .then_inc(mk_out, 16)

            mem_w_hi(N_MEM)
            mem_w_hi(N_MEM + 1)
            root(tools_x, 0)
            for c in range(KC):
                for kv in range(2):
                    slot, use = weight_turn(N_MEM + 2 * c + kv)
                    act.wait_ge(w_used[slot], use)
                    if kv == 0:
                        act.activation(mk_T[:, c, :], bank[0][:, 0:NM], ACT.Copy)
                    act.activation(m_kv[c % 2][kv][:, :], bank[kv][:, 0:NM], ACT.Copy).then_inc(m_read, 1)
                    if c < KC - 1:
                        mem_w_hi(N_MEM + 2 * c + kv + 2)
                hi_part(tools_x, 0, c)
                if c:
                    store_keys(c - 1)
            store_keys(KC - 1)
            for v in range(XH * QT + 4):
                if v < XH * QT:
                    act.wait_ge(xmx_done, 2 * v + 2)
                    if v >= 2:
                        act.wait_ge(xt_turned, v - 1)
                        act.wait_ge(xn_done, 2 * (v - 1))
                    act.activation(xp[v % 2][:, :], bank[v % 2][:, 0:NM], ACT.Exp, bias=xmx[:, v % 2:v % 2 + 1],
                                   accum_out=xrs[:, v % 2:v % 2 + 1]).then_inc(xe_done, 1)
                if 2 <= v < XH * QT + 2:
                    u = v - 2
                    hf = u // 4
                    act.wait_ge(xt_turned, u + 1)
                    if hf >= 2 and u % 4 == 0:
                        act.wait_ge(xv_ready, 2 * (hf - 1))
                    act.activation(xp_T[hf % 2][:, :, (u % 4) * P:(u % 4 + 1) * P],
                                   bank[2 + u % 2][:, 0:NM].rearrange("p (m n) -> p m n", m=2), ACT.Copy)\
                       .then_inc(xt_done, 1)
                if v >= 4 and (v - 4) % 4 == 3:
                    hf = (v - 4) // 4
                    for c in range(2):
                        act.wait_ge(xv_ready, 2 * hf + c + 1)
                        act.activation(g_hi[:, 2 * (hf // 2) + c, 512 * (hf % 2):512 * (hf % 2) + 512],
                                       bank[4 + 2 * (hf % 2) + c][:, :], ACT.Copy).then_inc(xv_hi, 1)
            act.wait_ge(xv_lo, 16)

            def keys_of(b):
                for h in (0, 2):
                    act.wait_ge(ct_turned[0], 2 * b + h // 2 + 1)
                    act.activation(ckt[0][:, :], bank[0][:, :], ACT.Copy).then_inc(ct_done[0], 1)

            def exp_of(e):
                act.wait_ge(c_dve, 2 * e + 2)
                act.activation(cs[e][:, :], bank[4 + e][:, 0:NM], ACT.Exp, bias=c_stat[:, e, 1:2],
                               accum_out=c_stat[:, e, 2:3]).then_inc(c_act, 1)

            def turned_of(e):
                act.wait_ge(c_turned, e + 1)
                act.activation(cp_T[e][:, :, :], bank[2 + e][:, 0:NM].rearrange("p (m n) -> p m n", m=2), ACT.Copy)\
                   .then_inc(c_act, 1)

            for b in range(4):
                keys_of(b)
            keys_of(4)
            exp_of(0)
            for b in range(5, NB):
                keys_of(b)
            turned_of(0)
            exp_of(1)
            for e in range(2):
                act.wait_ge(c_dve, 5 + e)
                act.wait_ge(co_ready, 8 * e + 7)
                act.activation(c_out[e][:, 0:512], bank[6][:, :], ACT.Copy, scale=c_stat[:, e, 3:4])\
                   .then_inc(co_done[0], 1)
                if e == 0:
                    turned_of(1)
            for e in range(2):
                for h in range(XH):
                    act.wait_ge(co_turned, 2 * e + h // 2 + 1)
                    act.activation(g_hi[:, 2 * h:2 * h + 2, TP + 32 * e:TP + 32 * e + 32]
                                   .rearrange("p c (b i) -> p c b i", b=4), own_head(h), ACT.Copy).then_inc(co_hi, 1)
            squares(tools_f, 1)
            root(tools_f, 1)
            for k in range(KC):
                hi_part(tools_f, 1, k)

            def tanhs(n, i=None):
                for ch in range(2):
                    slot, _ = weight_turn(n + 2 * ch)
                    for g, (t0, w) in enumerate(GROUPS):
                        base = 4 if i is not None else 0
                        q = 2 * (base + 2 * ch) + g + 1
                        if g < 2:
                            act.wait_ge(f_ready, q if i is None else 8 * i + q)
                        else:
                            slot, use = weight_turn(n + 2 * ch, i, 6)
                            act.wait_ge(w_used[slot], use)
                        ev = 3 * ((2 if i is not None else 0) + ch - 1) + g + 1
                        if ev > 0:
                            act.wait_ge(f_gate, ev if i is None else 6 * i + ev)
                        act.activation(f_th[:, t0:t0 + w], bank[g][:, 0:w], ACT.Tanh, scale=0.5)\
                           .then_inc(f_tanh, 1)

            def act_hi_parts(i=None):
                if i is not None:
                    act.wait_ge(d_added, 24 * i + 26)
                for ch in range(2):
                    act.wait_ge(f_gated, 3 * ch + 3 if i is None else 6 * i + (6 + 3 * ch + 3))
                    act.activation(act_hi[:, ch, :], gated[:, ch, :], ACT.Copy).then_inc(f_hi, 1)

            tanhs(N_FFN)
            act_hi_parts()
            with act.Fori(0, FFT - 1) as i:
                tanhs(N_FFN + 4, i)
                act_hi_parts(i)
            for k in range(KC):
                act.wait_ge(d_added, 24 * (FFT - 1) + 2 + 3 * (k + 1))
                if k >= 2:
                    act.wait_ge(r_summed, 18 + k)
                act.activation(tools_f["sq"][k % 2][:, :], xT[:, k, :], ACT.Square).then_inc(r_squared, 1)
                act.wait_ge(r_squared, 2 * KC + k + 1)
                act.activation(xT[:, k, :], xT[:, k, :], ACT.Copy, scale=gains[:, 2 * KC + k:2 * KC + k + 1])\
                   .then_inc(y_scaled, 1)
            root(tools_f, 2)
            for t in range(QT + 1):
                n = P if t < QT else TS
                act.wait_ge(y_turned, 2 * t + 1)
                if t == 0:
                    act.wait_ge(n_rinv, 6)
                act.activation(y_nat[t][0:n, 0:512], (bank[0], bank[2])[t % 2][0:n, :], ACT.Copy,
                               scale=tools_f["rinv"][0:n, t:t + 1])\
                   .then_inc(y_done[0], 1)

        @block.vector
        def _(dve):
            def tab(ins):
                ins.then_inc(tab_step, 1)
                steps[0] += 1
                dve.wait_ge(tab_step, steps[0])

            steps = [0]
            dve.memset(u_p[:, :, :], 0.0).then_inc(dve_step, 1)
            dve.memset(u_s[:, :, :, :], 0.0).then_inc(dve_step, 1)
            dve.wait_ge(tab_loaded, 16)
            starts = bucket_starts()
            tab(dve.memset(g_tab[:, :], MASKED))
            dve.tensor_copy(f_tab[:, 0:16], table[:, 0:16]).then_inc(tab_step, 1)
            steps[0] += 1
            for b in range(16, 32):
                a, z = starts[b], starts[b + 1]
                last = dve.tensor_copy(f_tab[:, a:z], table[:, b:b + 1].to_broadcast([NH, z - a]))
                if b < 31:
                    last.then_inc(tab_step, 1)
                    steps[0] += 1
            tab(last)
            for lo, hi, step, count in ((0, 128, 1, 1), (0, 128, 4, 2), (0, 128, 16, 3), (132, 512, 4, 1),
                                        (144, 512, 16, 2), (528, 2048, 16, 1)):
                tab(dve.tensor_scalar(g_tab[:, ZERO + lo:ZERO + hi + 1:step], f_tab[:, lo:hi + 1:step],
                                      math.log(count), None, ALU.add))
            dve.wait_ge(pool_step, 5)
            dve.wait_ge(vec_turned, 1)
            dve.tensor_copy(conv_vec[:, :, :], bank[7][:, 0:128].rearrange("p (c j) -> p c j", c=2)[:, :, 0:35])\
               .then_inc(dve_step, 1)
            dve.tensor_copy(gains[:, :], bank[7][:, 128:152]).then_inc(dve_step, 1)
            dve.wait_ge(dve_step, 4)
            dve.wait_ge(vec_turned, 2)
            dve.wait_ge(dve_step, 2)
            for g in range(2):
                for c in range(2):
                    last = dve.tensor_copy(u_s[:, c, 4 * g:4 * g + 4, 0:HIST],
                                           bank[2][:, 120 * (2 * g + c):120 * (2 * g + c) + 120]
                                           .rearrange("p (b j) -> p b j", b=4))
            last.then_inc(dve_step, 1)
            dve.wait_ge(gmix_loaded, 16)

            def lo_part(t):
                n = P if t < QT else TS
                for j in range(2):
                    dve.wait_ge(hi_done, 2 * t + j + 1)
                    src = bank[3 + 2 * (t % 2) + j][:, :].rearrange("p (k n) -> p k n", k=4)[:, :, 0:n]
                    dve.tensor_tensor(h_lo[:, 4 * j:4 * j + 4, t * P:t * P + n], src,
                                      h_hi[:, 4 * j:4 * j + 4, t * P:t * P + n].bitcast(F32),
                                      ALU.subtract).then_inc(lo_done, 1)

            for t in range(QT + 1):
                p, rows = t % 2, (P if t < QT else TS)
                dve.wait_ge(x_rms, 2 * t + 2)
                dve.reciprocal(rinv[0:rows, p:p + 1], rms[0:rows, p:p + 1]).then_inc(x_rinv, 1)
                dve.wait_ge(x_rinv, t + 1)
                dve.scalar_tensor_tensor(out=x_sc[p][0:rows, :], in0=x_nat[p][0:rows, :],
                                         scalar=rinv[0:rows, p:p + 1], in1=g_mix[0:rows, :],
                                         op0=ALU.mult, op1=ALU.mult).then_inc(x_scaled, 1)
                if t:
                    lo_part(t - 1)
            lo_part(QT)
            for c in range(2):
                for g, (t0, w) in enumerate(GROUPS):
                    dve.wait_ge(a_done, 3 * c + g + 1)
                    dve.wait_ge(t_done, 3 * c + g + 1)
                    t1 = min(t0 + w, TP)
                    last = dve.scalar_tensor_tensor(out=u_p[:, c, HIST + t0:HIST + t1], in0=tanh_g[:, t0:t1],
                                                    scalar=1.0, in1=a_half[:, t0:t1], op0=ALU.add, op1=ALU.mult)
                    if g == 2:
                        last = dve.scalar_tensor_tensor(out=u_new[:, c, :], in0=tanh_g[:, TP:T], scalar=1.0,
                                                        in1=a_half[:, TP:T], op0=ALU.add, op1=ALU.mult)
                    last.then_inc(u_done, 1)
            dve.wait_ge(u_done, 6)
            for c in range(2):
                dve.tensor_copy(u_s[:, c, :, HIST:HIST + NI], u_new[:, c, :].rearrange("p (b i) -> p b i", b=NB))\
                   .then_inc(dve_step, 1)
            dve.wait_ge(dve_step, 7)
            for c in range(2):
                dve.tensor_copy(y_conv[:, c, :], conv_vec[:, c, 32:33].to_broadcast([P, T]))\
                   .then_inc(conv_done, 1)
            dve.wait_ge(s1a_over, 1)
            dve.wait_ge(pool_step, 6)

            def read_qkv(pair, m):
                which, g = divmod(m, 3)
                t0, w = GROUPS[g]
                slot, use = pair.weights(which)
                if g < 2:
                    dve.wait_ge(qkv_ready, pair.at(6, 2 * which + g + 1))
                else:
                    dve.wait_ge(w_used[slot], use)
                src = bank[g][:, 0:w]
                if which == 0:
                    dve.tensor_copy(v_T[:, t0:t0 + w], src).then_inc(qkv_done, 1)
                elif which == 1:
                    if g == 2:
                        dve.tensor_copy(ks_T[:, pair.c, :], src[:, LAST_P:w])
                    dve.tensor_copy(k_T[pair.slot][:, t0:t0 + w], src).then_inc(qkv_done, 1)
                elif g < 2:
                    dve.tensor_scalar(q_T[pair.slot][:, t0:t0 + w], src, HD ** -0.5, None, ALU.mult)\
                       .then_inc(qkv_done, 1)
                else:
                    dve.tensor_scalar(q_T[pair.slot][:, t0:TP], src[:, 0:LAST_P], HD ** -0.5, None, ALU.mult)
                    for hh in range(2):
                        half = slice(HD * hh, HD * hh + HD)
                        last = dve.tensor_scalar(q_blk[half, :, pair.c, NI * hh:NI * hh + NI],
                                                 src[half, LAST_P:w].rearrange("p (b i) -> p b i", b=NB),
                                                 HD ** -0.5, None, ALU.mult)
                    last.then_inc(qkv_done, 1)

            def read_kv(pair, j):
                t0, t1 = TURNS[j % 3]
                dve.wait_ge(kv_turned, pair.at(6, j + 1))
                if j == 0 and not pair.first(1, -1):
                    dve.wait_ge(v_out[pair.slot], 16 * ((pair.c0) // 2) if pair.i is None
                                else 16 * (pair.c0 // 2) + 16 * pair.i)
                if j == 3 and not pair.first(1, 0):
                    dve.wait_ge(k_out, pair.at(16, 0))
                dst, new = (v_nat[pair.slot], vs_nat) if j < 3 else (k_nat, ks_nat)
                full = min(t1, QT)
                last = dve.tensor_copy(dst[:, t0:full, :],
                                       bank[7][:, P:P * (1 + full - t0)].rearrange("p (t c) -> p t c", c=P))
                if t1 > QT:
                    last = dve.tensor_copy(new[:, bass.ts(pair.c, P)], bank[7][0:TS, P * 3:P * 4])
                last.then_inc(kv_done, 1)

            def read_att(pair, j):
                t0, t1 = ATT_TURNS[j]
                dve.wait_ge(at_turned, pair.at(3, j + 1))
                dve.tensor_copy(xT[:, pair.c, t0 * P:t1 * P], bank[7][:, P:P * (1 + t1 - t0)]).then_inc(at_done, 1)

            def bias_scores(pair, s):
                hh, qb = UNITS[s]
                if s % 8 == 0:
                    dve.wait_ge(strip_loaded[hh], pair.at(16, 16))
                if not pair.first(16, s - 1):
                    dve.wait_ge(pv_done, pair.at(16, s - 1))
                chunks = 1 + (qb >= 4)
                for j in range(chunks):
                    n = min(512, unit_keys(s) - 512 * j)
                    dve.wait_ge(sc_ready[j], pair.at(16, s + 1) if j == 0 else pair.at(8, 4 * hh + qb - 3))
                    dve.sem_inc(tick, 1)
                    first = P * (qb + 1) - 512 * j
                    dve.tensor_tensor_reduce(out=sp[s % 2][:, 512 * j:512 * j + n], in0=bank[3 + j][:, 0:n],
                                             in1=strip[hh][:, first:first - n:-1], scale=1.0, scalar=LOWEST,
                                             op0=ALU.add, op1=ALU.max,
                                             accum_out=smax[:, s % 2, j:j + 1]).then_inc(sc_free[j], 1)
                dve.wait_ge(sc_free[chunks - 1], pair.at(16, s + 1) if chunks == 1 else pair.at(8, 4 * hh + qb - 3))
                if chunks == 1:
                    dve.tensor_scalar(nmax[:, s % 2:s % 2 + 1], smax[:, s % 2, 0:1], -1.0, None, ALU.mult)\
                       .then_inc(nm_ready, 1)
                else:
                    dve.tensor_scalar(nmax[:, s % 2:s % 2 + 1], smax[:, s % 2, 0:1], smax[:, s % 2, 1:2], -1.0,
                                      ALU.max, ALU.mult).then_inc(nm_ready, 1)

            def normalise(pair, s):
                hh, qb = UNITS[s]
                dve.wait_ge(pv_done, pair.at(16, s + 1))
                dve.reciprocal(rrec[:, s % 2:s % 2 + 1], rsum[:, s % 2:s % 2 + 1]).then_inc(rr_done, 1)
                dve.wait_ge(rr_done, pair.at(16, s + 1))
                dve.tensor_scalar(att[:, qb, HD * hh:HD * hh + HD], bank[7][:, HD * (s % 2):HD * (s % 2) + HD],
                                  rrec[:, s % 2:s % 2 + 1], None, ALU.mult).then_inc(norm_done, 1)

            def conv_tap(pair, s):
                c = s % 2
                tap = pair.at(8, s // 2 - 8)
                w = conv_vec[:, c, bass.ds(tap, 1)]
                for part in range(2):
                    dve.wait_ge(conv_done, pair.at(32, 2 * s + part - 32 + 1))
                    if part == 0:
                        y, u = y_conv[:, c, 0:TP], u_p[:, c, bass.ds(tap, TP)]
                    else:
                        y = y_conv[:, c, TP:T].rearrange("p (b i) -> p b i", b=NB)
                        u = u_s[:, c, :, bass.ds(tap, NI)]
                    dve.scalar_tensor_tensor(out=y, in0=u, scalar=w, in1=y, op0=ALU.mult, op1=ALU.add)\
                       .then_inc(conv_done, 1)

            def attend(pair, before=True, ahead=True, conv=False):
                for s in range(SLOTS):
                    if s < 16:
                        bias_scores(pair, s)
                    if before and s in att_slot:
                        read_att(Pair(pair.c0 - 1, pair.i), att_slot[s])
                    if ahead and s in kv_slot:
                        read_kv(pair.next(), kv_slot[s])
                    if ahead:
                        for m in ends_in[s]:
                            read_qkv(pair.next(), m)
                    if conv and s < 16:
                        conv_tap(pair, s)
                    if s >= 1:
                        normalise(pair, s - 1)

            for m in range(3):
                read_qkv(Pair(0), m)
            read_qkv(Pair(0), 3)
            for j in range(3):
                read_kv(Pair(0), j)
            for m in range(4, 9):
                read_qkv(Pair(0), m)
            for j in range(3, 6):
                read_kv(Pair(0), j)
            attend(Pair(0), before=False)
            with dve.Fori(0, 2) as i:
                attend(Pair(1, i), conv=True)
                attend(Pair(2, i), conv=True)
            attend(Pair(5), ahead=False)
            for j in range(3):
                read_att(Pair(5), j)
            for c in range(2):
                last = dve.tensor_scalar(half_vec[:, c, :], conv_vec[:, c, 33:35], 0.5, None, ALU.mult)
            dve.wait_ge(conv_done, 2 + 32 * 4)
            last.then_inc(ln_step, 1)
            for c in range(2):
                for g, (t0, n) in enumerate(GROUPS):
                    dve.wait_ge(ln_sums, g + 1)
                    dve.scalar_tensor_tensor(out=y_conv[:, c, t0:t0 + n], in0=bank[g][:, 0:n], scalar=-1.0 / CW,
                                             in1=y_conv[:, c, t0:t0 + n], op0=ALU.mult, op1=ALU.add)\
                       .then_inc(ln_step, 1)
            for g, (t0, n) in enumerate(GROUPS):
                dve.wait_ge(ln_act, 2 + g + 1)
                dve.reciprocal(ln_sd[:, t0:t0 + n], ln_sd[:, t0:t0 + n]).then_inc(ln_step, 1)
            dve.wait_ge(ln_step, 10)
            for c in range(2):
                for g, (t0, n) in enumerate(GROUPS):
                    dve.tensor_tensor(y_conv[:, c, t0:t0 + n], y_conv[:, c, t0:t0 + n], ln_sd[:, t0:t0 + n],
                                      ALU.mult).then_inc(ln_step, 1)
            for c in range(2):
                for g, (t0, n) in enumerate(GROUPS):
                    dve.wait_ge(ln_act, 5 + 2 * (3 * c + g) + 2)
                    dve.scalar_tensor_tensor(out=y_conv[:, c, t0:t0 + n], in0=ln_th[:, c, t0:t0 + n], scalar=1.0,
                                             in1=ln_sq[:, c, t0:t0 + n], op0=ALU.add, op1=ALU.mult)\
                       .then_inc(ln_step, 1)
            dve.wait_ge(strip_s, 16 * NH)
            dve.tensor_copy(d_row[:, 0:FAR * P].rearrange("p (j r) -> p j r", r=8),
                            d_strip[:, BUF + NI - 1:BUF + NI - 1 - NEAR0:-1]
                            .rearrange("p (j r) -> p j r", r=16)[:, :, 0:8])
            dve.tensor_copy(d_row[:, FAR * P:KT * P], d_strip[:, 7 + NEAR * P:7:-1])
            for p in range(2):
                dve.memset(q_pad[p][:, :], 0.0)
            dve.memset(d_new[:, :], MASKED).then_inc(d_made, 1)
            dve.wait_ge(d_made, 1)
            dve.tensor_copy(d_new[:, 56:56 + NI], d_strip[:, 7::-1]).then_inc(d_made, 1)
            dve.wait_ge(d_made, 2)

            def s_at(b0, i, per, count):
                fixed = per * b0 + count
                return fixed if i is None else fixed + 2 * per * i

            def queries(b0, i=None):
                b = b0 if i is None else b0 + 2 * i
                if b0 >= 2:
                    dve.wait_ge(st_ready, s_at(b0, i, 3, -3))
                dve.tensor_copy(q_pad[b0 % 2][:, :].rearrange("p (c r) -> p c r", c=PAIRS)[:, :, 0:16],
                                q_blk[:, bass.ds(b, 1), :, :]).then_inc(qp_ready, 1)

            def front(b0, i=None, ahead=True):
                p = b0 % 2
                b = b0 if i is None else b0 + 2 * i
                if b0:
                    dve.wait_ge(sr_done, s_at(b0, i, 3, 0))
                dve.tensor_copy(d_row[:, KT * P:], d_new[:, bass.ds(56 - NI * b, TS)]).then_inc(d_made, 1)
                for q in range(1, 22, 2):
                    if q < 18:
                        n = 512 if q < 12 else 256
                        dve.wait_ge(kt_turned[1], s_at(b0, i, 9, q // 2 + 1))
                        dve.tensor_copy(kt[1][:, 0:n], bank[1][:, 0:n]).then_inc(kt_done[1], 1)
                    if q == 5 and b0 >= 2:
                        read_out(b0 - 2, i)
                    if q in (7, 13, 19):
                        j = q // 6 - 1
                        if j == 0 and b0 >= 2:
                            dve.wait_ge(spt_turned[2], s_at(b0, i, 1, -1))
                        if j == 2:
                            dve.wait_ge(d_made, s_at(b0, i, 1, 3))
                        n = 512 if j < 2 else 256 + TS
                        dve.wait_ge(st_ready, s_at(b0, i, 3, j + 1))
                        dve.sem_inc(tick, 1)
                        dve.tensor_tensor_reduce(out=srow[p][:, j * 512:j * 512 + n], in0=bank[2 + j][0:96, 0:n],
                                                 in1=d_row[:, j * 512:j * 512 + n], scale=1.0, scalar=LOWEST,
                                                 op0=ALU.add, op1=ALU.max,
                                                 accum_out=smx[:, p, j:j + 1]).then_inc(sr_done, 1)
                dve.wait_ge(sr_done, s_at(b0, i, 3, 3))
                dve.tensor_reduce(smx[:, p, 6:7], smx[:, p, 0:3], AX.X, ALU.max).then_inc(snm_done, 1)
                dve.wait_ge(snm_done, s_at(b0, i, 2, 1))
                dve.tensor_scalar(snm[:, p:p + 1], smx[:, p, 6:7], -1.0, None, ALU.mult).then_inc(snm_done, 1)

            def turned_probs(b0, i=None):
                dve.wait_ge(spt_turned[1], s_at(b0, i, 1, 1))
                dve.tensor_copy(pT_s[:, 5:10, :], bank[2][:, 0:480].rearrange("p (k n) -> p k n", k=5))\
                   .then_inc(spt_done[1], 1)
                dve.wait_ge(sx_done, s_at(b0, i, 1, 1))
                dve.reciprocal(srr[:, b0 % 2:b0 % 2 + 1], srs[:, b0 % 2:b0 % 2 + 1]).then_inc(srr_done, 1)

            def scale_out(b0, i=None):
                p = b0 % 2
                dve.wait_ge(srr_done, s_at(b0, i, 1, 1))
                dve.wait_ge(ov_ready, s_at(b0, i, 2, 2))
                dve.tensor_scalar(o_sb[:, AW // 2:AW], bank[6][0:96, 0:AW // 2], srr[:, p:p + 1], None, ALU.mult)\
                   .then_inc(ov_done[1], 1)

            def read_out(b0, i=None):
                b = b0 if i is None else b0 + 2 * i
                for e in range(2):
                    dve.wait_ge(so_ready, s_at(b0, i, 2, e + 1))
                    for hh in range(2):
                        half = slice(HD * hh, HD * hh + HD)
                        first = 48 * e + NI * hh
                        dve.tensor_copy(xT[half, 3 * e:3 * e + 3, bass.ds(TP + NI * b, NI)],
                                        bank[(7, 3)[e]][half, 0:336].rearrange("p (c r) -> p c r", c=3)
                                        [:, :, first:first + NI]).then_inc(so_done, 1)

            queries(0)
            queries(1)
            front(0)
            front(1)
            turned_probs(0)
            scale_out(0)
            with dve.Fori(0, NB // 2 - 1) as i:
                queries(2, i)
                front(2, i)
                turned_probs(1, i)
                queries(3, i)
                scale_out(1, i)
                front(3, i)
                turned_probs(2, i)
                scale_out(2, i)
            read_out(NB - 2)
            turned_probs(NB - 1)
            scale_out(NB - 1)
            read_out(NB - 1)
            for k in range(KC):
                dve.wait_ge(n_hi, k + 1)
                dve.tensor_tensor(g_lo[:, k, :], xT[:, k, :], g_hi[:, k, :].bitcast(F32), ALU.subtract)\
                   .then_inc(n_lo, 1)
            dve.wait_ge(n_lo, KC)
            for t in range(QT + 1):
                n = P if t < QT else TS
                dve.wait_ge(xr_turned, 2 * t + 2)
                dve.tensor_copy(xT[:, 4:8, t * P:t * P + n],
                                bank[4 + 2 * (t % 2)][:, :].rearrange("p (k n) -> p k n", k=4)[:, :, 0:n])\
                   .then_inc(xr_done[1], 1)

            def add_residual(n0, tools, turn):
                dve.memset(tools["acc"][:, :], 0.0).then_inc(r_summed, 1)
                dve.sem_inc(r_added, 6)
                with dve.Fori(0, KC // 2) as i:
                    for s in range(2):
                        slot, use = weight_turn(n0 + s, i, 2)
                        for g, (t0, n) in enumerate(GROUPS):
                            if g < 2:
                                dve.wait_ge(r_ready, 4 * i + (16 * turn + 2 * s + g + 1))
                            else:
                                dve.wait_ge(w_used[slot], use)
                            place = xT[:, 2 * i + s, t0:t0 + n]
                            dve.tensor_tensor(place, bank[3 * s + g][:, 0:n], place, ALU.add)\
                               .then_inc(r_added, 1)
                        dve.wait_ge(r_squared, 2 * i + (KC * turn + s + 1))
                        dve.wait_ge(r_summed, 2 * i + ((KC + 1) * turn + s + 1))
                        dve.tensor_tensor(tools["acc"][:, :], tools["acc"][:, :], tools["sq"][s][:, :], ALU.add)\
                           .then_inc(r_summed, 1)

            def inverse_roots(tools, turn):
                dve.wait_ge(n_rms, 2 * turn + 2)
                for a, z, n in ((0, QT, P), (QT, QT + 1, TS)):
                    dve.reciprocal(tools["rinv"][0:n, a:z], tools["rms"][0:n, a:z]).then_inc(n_rinv, 1)
                dve.wait_ge(n_rinv, 2 * turn + 2)

            def diagonals(tools, turn):
                for t in range(QT + 1):
                    n = P if t < QT else TS
                    dve.tensor_scalar(tools["diag"][0:n, t, 0:n], ident[0:n, 0:n], tools["rinv"][0:n, t:t + 1], None,
                                      ALU.mult).then_inc(n_diag, 1)

            def norm_chunk(tools, turn, k):
                if k == 0:
                    dve.wait_ge(n_bc, 3 * turn + 3)
                if k >= 2 and turn < 2:
                    dve.wait_ge(n_lo, KC * (turn + 1) + k - 1)
                for g, (t0, n) in enumerate(TOKEN_BANKS):
                    x = xT[:, k, t0:t0 + n]
                    dve.scalar_tensor_tensor(out=x if turn == 2 else tools["tmp"][k % 2][:, t0:t0 + n], in0=x,
                                             scalar=gains[:, KC * turn + k:KC * turn + k + 1],
                                             in1=bank[3 + g][:, 0:n],
                                             op0=ALU.mult, op1=ALU.mult).then_inc(n_tmp, 1)

            def norm_lo(tools, turn, k):
                dve.wait_ge(n_hi, KC * (turn + 1) + k + 1)
                dve.tensor_tensor(g_lo[:, k, :], tools["tmp"][k % 2][:, :], g_hi[:, k, :].bitcast(F32),
                                  ALU.subtract).then_inc(n_lo, 1)

            def read_mem(c):
                dve.wait_ge(m_kv_turned, 2 * c + 1)
                if c:
                    dve.wait_ge(mk_out, 16 * c)
                dve.tensor_copy(mk_nat, bank[2][:, 0:NM].rearrange("p (t c) -> p t c", t=2))\
                   .then_inc(m_kv_done, 1)
                dve.wait_ge(m_kv_turned, 2 * c + 2)
                dve.tensor_copy(mv_nat[:, :, c * P:(c + 1) * P],
                                bank[6][:, 0:NM].rearrange("p (t c) -> p t c", t=2)).then_inc(m_kv_done, 1)

            dve.wait_ge(m_in, 48)
            dve.wait_ge(m_step, 4)
            dve.reciprocal(m_rinv, m_rms).then_inc(m_step, 1)
            dve.wait_ge(m_step, 5)
            for t in range(2):
                dve.scalar_tensor_tensor(out=mn[:, t, :], in0=mn[:, t, :],
                                         scalar=m_rinv[:, t:t + 1], in1=tools_x["tmp"][1][:, 0:D],
                                         op0=ALU.mult, op1=ALU.mult).then_inc(m_step, 1)
            add_residual(N_OUT, tools_x, 0)
            for t in range(2):
                for j in range(2):
                    dve.wait_ge(m_hi_done, 2 * t + j + 1)
                    at = (slice(None), slice(4 * j, 4 * j + 4), slice(t * P, (t + 1) * P))
                    dve.tensor_tensor(m_lo[at], (bank[0], bank[1], bank[2], bank[6])[2 * t + j][:, :]
                                      .rearrange("p (k n) -> p k n", k=4), m_hi[at].bitcast(F32), ALU.subtract)\
                       .then_inc(m_lo_done, 1)
            inverse_roots(tools_x, 0)
            diagonals(tools_x, 0)
            dve.sem_inc(m_kv_done, 2)
            for k in range(KC):
                norm_chunk(tools_x, 0, k)
                if k:
                    norm_lo(tools_x, 0, k - 1)
                    read_mem(k - 1)
            norm_lo(tools_x, 0, KC - 1)
            read_mem(KC - 1)
            dve.wait_ge(mk_out, 16 * KC)
            dve.sem_inc(xq_done, 6)
            with dve.Fori(0, KC // 2) as i:
                for s in range(2):
                    slot, use = weight_turn(N_XQ + s, i, 2)
                    for g, (t0, n) in enumerate(GROUPS):
                        if g < 2:
                            dve.wait_ge(xq_ready, 4 * i + (2 * s + g + 1))
                        else:
                            dve.wait_ge(w_used[slot], use)
                            dve.tensor_scalar(qx_s[:, 2 * i + s, :], bank[3 * s + g][:, LAST_P:n], XD ** -0.5, None,
                                              ALU.mult)
                        t1 = min(t0 + n, TP)
                        dve.tensor_scalar(qx[:, 2 * i + s, t0:t1], bank[3 * s + g][:, 0:t1 - t0], XD ** -0.5, None,
                                          ALU.mult).then_inc(xq_done, 1)
            for v in range(XH * QT + 5):
                if v < XH * QT:
                    dve.wait_ge(xs_ready, v + 1)
                    dve.tensor_reduce(xm[:, v % 2:v % 2 + 1], bank[v % 2][:, 0:NM], AX.X, ALU.max)\
                       .then_inc(xmx_done, 1)
                    dve.wait_ge(xmx_done, 2 * v + 1)
                    dve.tensor_scalar(xmx[:, v % 2:v % 2 + 1], xm[:, v % 2:v % 2 + 1], -1.0, None, ALU.mult)\
                       .then_inc(xmx_done, 1)
                if 1 <= v < XH * QT + 1:
                    u = v - 1
                    at = slice(u % 2, u % 2 + 1)
                    dve.wait_ge(xe_done, u + 1)
                    dve.reciprocal(xrr[:, at], xrs[:, at]).then_inc(xn_done, 1)
                    dve.wait_ge(xn_done, 2 * u + 1)
                    dve.tensor_scalar(xp[u % 2][:, :], xp[u % 2][:, :], xrr[:, at], None, ALU.mult)\
                       .then_inc(xn_done, 1)
                if v >= 5 and (v - 5) % 4 == 3:
                    hf = (v - 5) // 4
                    for c in range(2):
                        dve.wait_ge(xv_hi, 2 * hf + c + 1)
                        at = (slice(None), 2 * (hf // 2) + c, slice(512 * (hf % 2), 512 * (hf % 2) + 512))
                        dve.tensor_tensor(g_lo[at], bank[4 + 2 * (hf % 2) + c][:, :], g_hi[at].bitcast(F32),
                                          ALU.subtract).then_inc(xv_lo, 1)
            def pad_queries(b):
                if b >= 2:
                    dve.wait_ge(cs_ready, b - 1)
                for c in range(2):
                    last = dve.tensor_copy(cq_pad[b % 2][:, 32 * c:32 * c + 288].rearrange("p (h r) -> p h r", h=XH)
                                           [:, :, 0:NI],
                                           qx_s[:, :, b * NI:(b + 1) * NI].rearrange("p (h c) i -> p h c i", c=2)
                                           [:, :, c, :])
                last.then_inc(cq_ready, 1)

            for p in range(2):
                last = dve.memset(cq_pad[p][:, :], 0.0)
            last.then_inc(c_zero, 1)
            dve.wait_ge(c_zero, 1)
            pad_queries(0)
            for b in range(NB):
                if b < NB - 1:
                    pad_queries(b + 1)
                for h in (1, 3):
                    dve.wait_ge(ct_turned[1], 2 * b + h // 2 + 1)
                    dve.tensor_copy(ckt[1][:, :], bank[1][:, :]).then_inc(ct_done[1], 1)
                if b % 4 == 3:
                    e = b // 4
                    dve.wait_ge(cs_ready, b + 1)
                    dve.tensor_reduce(c_stat[:, e, 0:1], bank[4 + e][:, 0:NM], AX.X, ALU.max).then_inc(c_dve, 1)
                    dve.wait_ge(c_dve, 2 * e + 1)
                    dve.tensor_scalar(c_stat[:, e, 1:2], c_stat[:, e, 0:1], -1.0, None, ALU.mult).then_inc(c_dve, 1)
            for e in range(2):
                dve.wait_ge(c_act, 2 * e + 1)
                dve.reciprocal(c_stat[:, e, 3:4], c_stat[:, e, 2:3]).then_inc(c_dve, 1)
                dve.wait_ge(c_dve, 5 + e)
                dve.wait_ge(co_ready, 8 * e + 8)
                dve.tensor_scalar(c_out[e][:, 512:D], bank[7][:, :], c_stat[:, e, 3:4], None, ALU.mult)\
                   .then_inc(co_done[1], 1)
            for e in range(2):
                for h in range(XH):
                    dve.wait_ge(co_hi, 4 * e + 2 * (h // 2) + 2)
                    at = (slice(None), slice(2 * h, 2 * h + 2), slice(TP + 32 * e, TP + 32 * e + 32))
                    dve.tensor_tensor(g_lo[at].rearrange("p c (b i) -> p c b i", b=4), own_head(h),
                                      g_hi[at].rearrange("p c (b i) -> p c b i", b=4).bitcast(F32), ALU.subtract)\
                       .then_inc(co_lo, 1)
            add_residual(N_XO, tools_f, 1)
            inverse_roots(tools_f, 1)
            diagonals(tools_f, 1)
            for k in range(KC):
                norm_chunk(tools_f, 1, k)
                if k:
                    norm_lo(tools_f, 1, k - 1)
            norm_lo(tools_f, 1, KC - 1)

            def gate(n, i=None):
                base = 0 if i is None else 4
                for ch in range(2):
                    for k in range(2):
                        slot, use = weight_turn(n + 2 * ch + k, i, 6)
                        for g, (t0, w) in enumerate(GROUPS):
                            ev = 3 * ((0 if i is None else 2) + ch) + g + 1
                            at = lambda v: v if i is None else 6 * i + v
                            out = gated[:, ch, t0:t0 + w]
                            if k == 0:
                                dve.wait_ge(f_tanh, at(ev))
                                if i is not None and ch == 0 and g == 0:
                                    dve.wait_ge(f_lo, 2 * i + 2)
                                dve.scalar_tensor_tensor(out=out, in0=f_th[:, t0:t0 + w], scalar=1.0,
                                                         in1=bank[g][:, 0:w], op0=ALU.add, op1=ALU.mult)\
                                   .then_inc(f_gate, 1)
                            else:
                                if g < 2:
                                    q = 2 * (base + 2 * ch + 1) + g + 1
                                    dve.wait_ge(f_ready, q if i is None else 8 * i + q)
                                else:
                                    dve.wait_ge(w_used[slot], use)
                                dve.wait_ge(f_gate, at(ev))
                                dve.scalar_tensor_tensor(out=out, in0=out, scalar=0.5, in1=bank[3 + g][:, 0:w],
                                                         op0=ALU.mult, op1=ALU.mult).then_inc(f_gated, 1)

            def rest_parts(i=None):
                for ch in range(2):
                    dve.wait_ge(f_hi, ch + 1 if i is None else 2 * i + (ch + 3))
                    dve.tensor_tensor(act_lo[:, ch, :], gated[:, ch, :], act_hi[:, ch, :].bitcast(F32), ALU.subtract)\
                       .then_inc(f_lo, 1)

            def sum_squares(k):
                dve.wait_ge(r_squared, 2 * KC + k + 1)
                dve.wait_ge(r_summed, 2 * (KC + 1) + k + 1)
                dve.tensor_tensor(tools_f["acc"][:, :], tools_f["acc"][:, :], tools_f["sq"][k % 2][:, :], ALU.add)\
                   .then_inc(r_summed, 1)

            def add_down(n, i=None):
                for r in range(24):
                    if i is None and r % 3 == 2 and r > 3:
                        sum_squares(r // 3 - 1)
                    k, rr = divmod(r, 12)
                    slot, use = weight_turn(n + k, i, 6)
                    if rr < 11:
                        c0 = 22 * (FFT - 1) if i is None else 0
                        at = c0 + 11 * k + rr + 1
                        dve.wait_ge(d_ready, at if i is None else 22 * i + at)
                    else:
                        dve.wait_ge(w_used[slot], use)
                    o, g = divmod(r, 3)
                    t0, w = GROUPS[g]
                    place = xT[:, o, t0:t0 + w]
                    dve.tensor_tensor(place, bank[6 + r % 2][:, 0:w], place, ALU.add).then_inc(d_added, 1)

            dve.sem_inc(d_added, 2)
            gate(N_FFN)
            rest_parts()
            with dve.Fori(0, FFT - 1) as i:
                gate(N_FFN + 4, i)
                add_down(N_FFN + 8, i)
                rest_parts(i)
            dve.memset(tools_f["acc"][:, :], 0.0).then_inc(r_summed, 1)
            add_down(N_FFN + 6 * FFT - 2)
            sum_squares(KC - 1)
            inverse_roots(tools_f, 2)
            for t in range(QT + 1):
                n = P if t < QT else TS
                dve.wait_ge(y_turned, 2 * t + 2)
                dve.tensor_scalar(y_nat[t][0:n, 512:D], (bank[1], bank[6])[t % 2][0:n, :],
                                  tools_f["rinv"][0:n, t:t + 1], None, ALU.mult)\
                   .then_inc(y_done[1], 1)


_INS = ['x_prompt', 'x_sample', 'mem_prompt', 'cache_win_k', 'cache_win_v', 'cache_conv', 'cache_mem_k',
        'cache_mem_v', 'rpb_table', 'norm_mix_g', 'w_in', 'conv_w', 'conv_b', 'conv_ln_g', 'conv_ln_b', 'w_out',
        'norm_x_g', 'norm_mem_g', 'w_xq', 'w_xk', 'w_xv', 'w_xo', 'norm_ffn_g', 'w_ffn_gate', 'w_ffn_up',
        'w_ffn_down', 'norm_final_g']
_OUTS = [('out_yp', (1, TP, D)), ('out_ys', (NB, NI, D)), ('out_pk', (1, 1, TP, NH, HD)),
         ('out_pv', (1, 1, TP, NH, HD)), ('out_conv_p', (1, 1, HIST, CW)), ('out_mk', (1, 1, NM, XH, XD)),
         ('out_mv', (1, 1, NM, XH, XD)), ('out_sk', (1, NB, BUF, NH, HD)), ('out_sv', (1, NB, BUF, NH, HD)),
         ('out_conv_s', (1, NB, HIST, CW))]
_VIEWS = {
    'x_prompt': "a t c -> (a t) c", 'x_sample': "b i c -> (b i) c", 'mem_prompt': "a t c -> (a t) c",
    'cache_win_k': "a b t h d -> (a b) t (h d)", 'cache_win_v': "a b t h d -> (a b) t (h d)",
    'cache_conv': "a b j c -> (a b j) c",
    'cache_mem_k': "a b t h d -> (a b) t (h d)", 'cache_mem_v': "a b t h d -> (a b) t (h d)",
    'w_in': "a k c -> (a k) c", 'conv_w': "a j c -> (a j) c", 'w_out': "a k c -> (a k) c",
    'w_xq': "a k c -> (a k) c", 'w_xk': "a k c -> (a k) c", 'w_xv': "a k c -> (a k) c",
    'w_xo': "a k c -> (a k) c", 'w_ffn_gate': "a k c -> (a k) c", 'w_ffn_up': "a k c -> (a k) c",
    'w_ffn_down': "a k c -> (a k) c",
    'norm_x_g': "a (k p) -> (a k) p", 'norm_ffn_g': "a (k p) -> (a k) p", 'norm_final_g': "(k p) -> k p",
    'out_yp': "a t c -> (a t) c", 'out_ys': "b i c -> (b i) c", 'out_pk': "a b t h d -> (a b t) (h d)",
    'out_pv': "a b t h d -> (a b t) (h d)", 'out_conv_p': "a b j c -> (a b j) c",
    'out_mk': "a b t h d -> (a b t) (h d)", 'out_mv': "a b t h d -> (a b t) (h d)",
    'out_sk': "a b t h d -> (a b) t (h d)", 'out_sv': "a b t h d -> (a b) t (h d)",
    'out_conv_s': "a b j c -> (a b) j c",
}


def kernel(**inputs):
    import numpy as _np
    import concourse.bacc as _bacc
    from concourse import mybir as _mybir
    from concourse.bass_utils import run_bass_kernel_spmd as _run

    nc = _bacc.Bacc("TRN2", target_bir_lowering=False, num_devices=1)
    arrays, views = {}, {}
    for name in _INS:
        a = _np.ascontiguousarray(inputs[name])
        arrays[f"in_{name}_dram"] = a
        views[name] = nc.dram_tensor(f"in_{name}_dram", a.shape, _mybir.dt.from_np(a.dtype),
                                     kind="ExternalInput").ap()
    for name, shape in _OUTS:
        views[name] = nc.dram_tensor(f"{name}_dram", shape, _mybir.dt.from_np(_np.dtype('float32')),
                                     kind="ExternalOutput").ap()
    views["cache_conv3"] = views["cache_conv"].rearrange("a b j c -> (a b) j c")
    for name, pattern in _VIEWS.items():
        views[name] = views[name].rearrange(pattern, **({"p": P} if "p)" in pattern else {}))
    views["g_scratch"] = nc.dram_tensor("g_scratch_dram", (NH, GL), _mybir.dt.float32).ap()
    layer_step(nc, views)
    r = _run(nc, [arrays], core_ids=[0])
    return tuple(r.results[0][f"{name}_dram"] for name, _ in _OUTS)
```
